# Optimizing a Trainium2 kernel written in Bass

```python
import jax, jax.numpy as jnp
from jax import lax
import numpy as np
import math

D_MODEL = 1024
BATCH = 1
SEQ = 256
DEPTH = 1

A_HEADS = 8
A_HEAD_DIM = 64
A_WIDTH = A_HEADS * A_HEAD_DIM
MOBA_BLOCK = 256
MOBA_TOPK = 3
MOBA_QCHUNK = 32
ROPE_THETA = 10000.0
B_HEADS = 4
B_HEAD_DIM = 128
B_WIDTH = B_HEADS * B_HEAD_DIM
MLSTM_CHUNK = 64
CONV_WIDTH = 4
D_FF = ((8 * D_MODEL + 3 * 256 - 1) // (3 * 256)) * 256
NORM_EPS = 1e-6

IN_SIZES = [A_WIDTH, A_WIDTH, A_WIDTH,
            2 * B_WIDTH,
            B_WIDTH, B_WIDTH,
            B_HEADS, B_HEADS,
            D_MODEL, D_MODEL]
IN_WIDTH = sum(IN_SIZES)
IN_SPLITS = [int(s) for s in np.cumsum(IN_SIZES)[:-1]]


def rms_norm(x, g):
    xf = x.astype(jnp.float32)
    y = xf * lax.rsqrt(jnp.mean(xf * xf, axis=-1, keepdims=True) + NORM_EPS)
    return (y * g.astype(jnp.float32)).astype(x.dtype)

def rope(x, pos):
    half = x.shape[-1] // 2
    inv = ROPE_THETA ** (-jnp.arange(half, dtype=jnp.float32) / half)
    ang = pos.astype(jnp.float32)[:, None] * inv[None, :]
    cos, sin = jnp.cos(ang), jnp.sin(ang)
    xf = x.astype(jnp.float32)
    x1, x2 = xf[..., :half], xf[..., half:]
    return jnp.concatenate([x1 * cos - x2 * sin, x2 * cos + x1 * sin], axis=-1).astype(x.dtype)

def causal_depthwise_conv(x, w):
    width, chans = w.shape
    return lax.conv_general_dilated(
        x, w[:, None, :].astype(x.dtype), window_strides=(1,),
        padding=((width - 1, 0),), dimension_numbers=('NWC', 'WIO', 'NWC'),
        feature_group_count=chans)

def moba_attention(q, k, v):
    bn, nh, s, dh = q.shape
    nb = -(-s // MOBA_BLOCK)
    sp = nb * MOBA_BLOCK
    pad = ((0, 0), (0, 0), (0, sp - s), (0, 0))
    q, k, v = jnp.pad(q, pad), jnp.pad(k, pad), jnp.pad(v, pad)
    kb = k.reshape(bn, nh, nb, MOBA_BLOCK, dh)
    vb = v.reshape(bn, nh, nb, MOBA_BLOCK, dh)
    scale = dh ** -0.5
    topk = min(MOBA_TOPK, nb - 1)
    nq = sp // MOBA_QCHUNK
    qc = jnp.moveaxis(q.reshape(bn, nh, nq, MOBA_QCHUNK, dh), 2, 0)
    starts = jnp.arange(nq) * MOBA_QCHUNK
    if topk > 0:
        kmean = kb.astype(jnp.float32).mean(axis=3)
        gate = jnp.einsum('bhsd,bhnd->bhsn', q.astype(jnp.float32), kmean)
        q_blk = jnp.arange(sp) // MOBA_BLOCK
        past = jnp.arange(nb)[None, :] < q_blk[:, None]
        gate = jnp.where(past, gate, -jnp.inf)
        top_val, top_idx = lax.top_k(gate, topk)
        valid = jnp.isfinite(top_val)
        idx_c = jnp.moveaxis(top_idx.reshape(bn, nh, nq, MOBA_QCHUNK, topk), 2, 0)
        val_c = jnp.moveaxis(valid.reshape(bn, nh, nq, MOBA_QCHUNK, topk), 2, 0)
        xs = (qc, starts, idx_c, val_c)
    else:
        xs = (qc, starts)
    bi = jnp.arange(bn)[:, None, None, None]
    hi = jnp.arange(nh)[None, :, None, None]

    def attend_chunk(args):
        qi, start = args[0], args[1]
        blk = start // MOBA_BLOCK
        k_own = lax.dynamic_index_in_dim(kb, blk, axis=2, keepdims=False)
        v_own = lax.dynamic_index_in_dim(vb, blk, axis=2, keepdims=False)
        qpos = start + jnp.arange(MOBA_QCHUNK)
        kpos = blk * MOBA_BLOCK + jnp.arange(MOBA_BLOCK)
        causal = kpos[None, :] <= qpos[:, None]
        s_own = jnp.einsum('bhqd,bhkd->bhqk', qi, k_own).astype(jnp.float32) * scale
        s_own = jnp.where(causal, s_own, -jnp.inf)
        if topk > 0:
            idx_i, valid_i = args[2], args[3]
            k_sel = kb[bi, hi, idx_i]
            v_sel = vb[bi, hi, idx_i]
            s_sel = jnp.einsum('bhqd,bhqrkd->bhqrk', qi, k_sel).astype(jnp.float32) * scale
            s_sel = jnp.where(valid_i[..., None], s_sel, -jnp.inf)
            s_sel = s_sel.reshape(bn, nh, MOBA_QCHUNK, topk * MOBA_BLOCK)
            p = jax.nn.softmax(jnp.concatenate([s_sel, s_own], axis=-1), axis=-1).astype(v.dtype)
            p_sel = p[..., :topk * MOBA_BLOCK].reshape(bn, nh, MOBA_QCHUNK, topk, MOBA_BLOCK)
            return (jnp.einsum('bhqrk,bhqrkd->bhqd', p_sel, v_sel)
                    + jnp.einsum('bhqk,bhkd->bhqd', p[..., topk * MOBA_BLOCK:], v_own))
        p = jax.nn.softmax(s_own, axis=-1).astype(v.dtype)
        return jnp.einsum('bhqk,bhkd->bhqd', p, v_own)

    out = lax.map(attend_chunk, xs)
    return jnp.moveaxis(out, 0, 2).reshape(bn, nh, sp, dh)[:, :, :s]

def mlstm_chunkwise(q, k, v, i_pre, f_pre):
    bn, nh, s, d = q.shape
    L = MLSTM_CHUNK
    nc = s // L
    f32 = jnp.float32
    q = q.astype(f32)
    k = k.astype(f32) * (d ** -0.5)
    v = v.astype(f32)
    log_f = jax.nn.log_sigmoid(f_pre.astype(f32))
    log_i = i_pre.astype(f32)

    def chunks(a):
        return jnp.moveaxis(a.reshape(bn, nh, nc, L, *a.shape[3:]), 2, 0)

    tri = jnp.tril(jnp.ones((L, L), dtype=bool))

    def step(carry, xs):
        C, n, m = carry
        qc, kc, vc, ic, fc = xs
        b = jnp.cumsum(fc, axis=-1)
        dmat = jnp.where(tri, b[..., :, None] - b[..., None, :] + ic[..., None, :], -jnp.inf)
        m_inter = b + m[..., None]
        m_t = jnp.maximum(m_inter, dmat.max(axis=-1))
        sc = jnp.einsum('bhtd,bhsd->bhts', qc, kc) * jnp.exp(dmat - m_t[..., None])
        w_inter = jnp.exp(m_inter - m_t)
        num = (jnp.einsum('bhts,bhse->bhte', sc, vc)
               + w_inter[..., None] * jnp.einsum('bhtd,bhde->bhte', qc, C))
        den = sc.sum(axis=-1) + w_inter * jnp.einsum('bhtd,bhd->bht', qc, n)
        h = num / jnp.maximum(jnp.abs(den), jnp.exp(-m_t))[..., None]
        b_tot = b[..., -1]
        g = b_tot[..., None] - b + ic
        m_new = jnp.maximum(b_tot + m, g.max(axis=-1))
        w_c = jnp.exp(b_tot + m - m_new)
        w_s = jnp.exp(g - m_new[..., None])
        C = w_c[..., None, None] * C + jnp.einsum('bhs,bhsd,bhse->bhde', w_s, kc, vc)
        n = w_c[..., None] * n + jnp.einsum('bhs,bhsd->bhd', w_s, kc)
        return (C, n, m_new), h

    init = (jnp.zeros((bn, nh, d, d), f32), jnp.zeros((bn, nh, d), f32), jnp.zeros((bn, nh), f32))
    _, hs = lax.scan(step, init, (chunks(q), chunks(k), chunks(v), chunks(log_i), chunks(log_f)))
    return jnp.moveaxis(hs, 0, 2).reshape(bn, nh, s, d)

def first_inputs(seed: int = 0) -> dict:
    key = jax.random.key(seed)
    ks = jax.random.split(key, 16)
    nrm = jax.random.normal
    f32 = jnp.float32
    return {
        "x": nrm(ks[0], (BATCH, SEQ, D_MODEL), f32),
        "norm_mix_g": 1.0 + 0.02 * nrm(ks[1], (DEPTH, D_MODEL), f32),
        "w_in": nrm(ks[2], (DEPTH, D_MODEL, IN_WIDTH), f32) * D_MODEL ** -0.5,
        "conv_w": nrm(ks[3], (DEPTH, CONV_WIDTH, 2 * B_WIDTH), f32) * CONV_WIDTH ** -0.5,
        "b_igate": 0.1 * nrm(ks[4], (DEPTH, B_HEADS), f32),
        "b_fgate": jnp.linspace(3.0, 6.0, B_HEADS, dtype=f32)[None, :] + 0.1 * nrm(ks[5], (DEPTH, B_HEADS), f32),
        "mlstm_norm_g": 1.0 + 0.02 * nrm(ks[6], (DEPTH, B_WIDTH), f32),
        "w_proj_a": nrm(ks[7], (DEPTH, A_WIDTH, D_MODEL), f32) * A_WIDTH ** -0.5,
        "w_proj_b": nrm(ks[8], (DEPTH, B_WIDTH, D_MODEL), f32) * B_WIDTH ** -0.5,
        "w_out": nrm(ks[9], (DEPTH, D_MODEL, D_MODEL), f32) * D_MODEL ** -0.5,
        "norm_ffn_g": 1.0 + 0.02 * nrm(ks[10], (DEPTH, D_MODEL), f32),
        "w_gate_up": nrm(ks[11], (DEPTH, D_MODEL, 2 * D_FF), f32) * D_MODEL ** -0.5,
        "w_down": nrm(ks[12], (DEPTH, D_FF, D_MODEL), f32) * D_FF ** -0.5,
        "norm_final_g": 1.0 + 0.02 * nrm(ks[13], (D_MODEL,), f32),
    }

def first_block(x, norm_mix_g, w_in, conv_w, b_igate, b_fgate, mlstm_norm_g, w_proj_a, w_proj_b,
              w_out, norm_ffn_g, w_gate_up, w_down, norm_final_g):
    bn, s, _ = x.shape
    pos = jnp.arange(s)

    def to_heads(t, nh):
        return t.reshape(bn, s, nh, -1).transpose(0, 2, 1, 3)

    h = x
    for l in range(DEPTH):
        u = rms_norm(h, norm_mix_g[l])
        z = u @ w_in[l]
        qa, ka, va, qk_b, vb, ob, ib, fb, ga, gb = jnp.split(z, IN_SPLITS, axis=-1)

        qa = rope(to_heads(qa, A_HEADS), pos)
        ka = rope(to_heads(ka, A_HEADS), pos)
        ya = moba_attention(qa, ka, to_heads(va, A_HEADS))
        ya = ya.transpose(0, 2, 1, 3).reshape(bn, s, A_WIDTH)

        qk_b = jax.nn.silu(causal_depthwise_conv(qk_b, conv_w[l]))
        qb, kb_ = jnp.split(qk_b, 2, axis=-1)
        i_pre = (ib + b_igate[l].astype(ib.dtype)).transpose(0, 2, 1)
        f_pre = (fb + b_fgate[l].astype(fb.dtype)).transpose(0, 2, 1)
        hb = mlstm_chunkwise(to_heads(qb, B_HEADS), to_heads(kb_, B_HEADS), to_heads(vb, B_HEADS),
                             i_pre, f_pre)
        hb = hb * lax.rsqrt(jnp.mean(hb * hb, axis=-1, keepdims=True) + NORM_EPS)
        hb = hb.transpose(0, 2, 1, 3).reshape(bn, s, B_WIDTH) * mlstm_norm_g[l].astype(jnp.float32)
        yb = (jax.nn.sigmoid(ob.astype(jnp.float32)) * hb).astype(u.dtype)

        merged = (jax.nn.sigmoid(ga) * (ya @ w_proj_a[l])
                  + jax.nn.sigmoid(gb) * (yb @ w_proj_b[l]))
        h = h + merged @ w_out[l]

        u = rms_norm(h, norm_ffn_g[l])
        g, up = jnp.split(u @ w_gate_up[l], 2, axis=-1)
        h = h + (jax.nn.silu(g) * up) @ w_down[l]

    return rms_norm(h, norm_final_g)


DEPTH_2 = 2

CHUNK = 64
HEAD_DIM = 64
N_SELF_HEADS = 12
N_DIFF_HEADS = 6
N_MEM_HEADS = 4
N_MEM = 256
SELF_WIDTH = N_SELF_HEADS * HEAD_DIM
MEM_WIDTH = N_MEM_HEADS * HEAD_DIM
IN_WIDTH_2 = 3 * SELF_WIDTH + MEM_WIDTH
LEFT_CHUNKS = 8
BAND = (LEFT_CHUNKS + 1) * CHUNK
REL_CLIP = 128
N_REL = 2 * REL_CLIP + 1
Q_BLOCK = 128
D_FF_2 = 2816
EPS = 1e-6
NEG_INF = -1e30
N_MIXERS = 2
N_A_LAYERS = (DEPTH_2 + 1) // 2
N_B_LAYERS = DEPTH_2 // 2


def rmsnorm(x, g):
    x32 = x.astype(jnp.float32)
    y = x32 * lax.rsqrt(jnp.mean(x32 * x32, axis=-1, keepdims=True) + EPS)
    return (y * g.astype(jnp.float32)).astype(x.dtype)

def swiglu(h, w_gate, w_up, w_down):
    return (jax.nn.silu(h @ w_gate) * (h @ w_up)) @ w_down

def rope_tables(positions):
    inv_freq = 1.0 / (ROPE_THETA ** (jnp.arange(0, HEAD_DIM, 2, dtype=jnp.float32) / HEAD_DIM))
    ang = positions.astype(jnp.float32)[..., None] * inv_freq
    return jnp.cos(ang), jnp.sin(ang)

def apply_rope(x, cos, sin):
    x32 = x.astype(jnp.float32)
    x1, x2 = jnp.split(x32, 2, axis=-1)
    return jnp.concatenate([x1 * cos - x2 * sin, x2 * cos + x1 * sin], axis=-1).astype(x.dtype)

def chunked_rel_attention(q, k, v, rel_bias):
    B, S, H, D = q.shape
    n_chunks = S // CHUNK
    pad = ((0, 0), (LEFT_CHUNKS * CHUNK, 0), (0, 0), (0, 0))
    kp = jnp.pad(k, pad)
    vp = jnp.pad(v, pad)
    qi = jnp.arange(CHUNK)[:, None]
    ks = jnp.arange(BAND)[None, :]
    rel = LEFT_CHUNKS * CHUNK + qi - ks
    bias = rel_bias[:, jnp.clip(rel, -REL_CLIP, REL_CLIP) + REL_CLIP].astype(jnp.float32)
    scale = HEAD_DIM ** -0.5
    slot = jnp.arange(BAND)

    def one_chunk(c):
        start = c * CHUNK
        qc = lax.dynamic_slice_in_dim(q, start, CHUNK, axis=1)
        kc = lax.dynamic_slice_in_dim(kp, start, BAND, axis=1)
        vc = lax.dynamic_slice_in_dim(vp, start, BAND, axis=1)
        s = jnp.einsum('bqhd,bkhd->bhqk', qc, kc).astype(jnp.float32) * scale + bias
        valid = slot >= (LEFT_CHUNKS - c) * CHUNK
        s = jnp.where(valid, s, NEG_INF)
        p = jax.nn.softmax(s, axis=-1).astype(v.dtype)
        return jnp.einsum('bhqk,bkhd->bqhd', p, vc)

    out = lax.map(one_chunk, jnp.arange(n_chunks))
    return out.transpose(1, 0, 2, 3, 4).reshape(B, S, H, D)

def diff_attention(q, k, v, lam):
    B, S, H, _, D = q.shape
    n_blocks = S // Q_BLOCK
    scale = D ** -0.5
    k_chunk = jnp.arange(S) // CHUNK
    qb = q.reshape(B, n_blocks, Q_BLOCK, H, 2, D).transpose(1, 0, 2, 3, 4, 5)

    def one_block(args):
        q_blk, b = args
        s = jnp.einsum('bqhcd,bkhcd->bhcqk', q_blk, k).astype(jnp.float32) * scale
        q_chunk = (b * Q_BLOCK + jnp.arange(Q_BLOCK)) // CHUNK
        allowed = k_chunk[None, :] <= q_chunk[:, None]
        s = jnp.where(allowed, s, NEG_INF)
        p = jax.nn.softmax(s, axis=-1)
        a = (p[:, :, 0] - lam * p[:, :, 1]).astype(v.dtype)
        return jnp.einsum('bhqk,bkhe->bqhe', a, v)

    out = lax.map(one_block, (qb, jnp.arange(n_blocks)))
    return out.transpose(1, 0, 2, 3, 4).reshape(B, S, H, v.shape[-1])

def memory_attention(q, k, v):
    s = jnp.einsum('bshd,bnhd->bhsn', q, k).astype(jnp.float32) * (HEAD_DIM ** -0.5)
    p = jax.nn.softmax(s, axis=-1).astype(v.dtype)
    return jnp.einsum('bhsn,bnhd->bshd', p, v)

def second_inputs(seed: int = 0) -> dict:
    key = jax.random.key(seed)
    ks = iter(jax.random.split(key, 40))
    f32 = jnp.float32

    def nrm(shape, scale):
        return jax.random.normal(next(ks), shape, f32) * scale

    def gain(shape):
        return 1.0 + 0.02 * jax.random.normal(next(ks), shape, f32)

    x = nrm((BATCH, SEQ, D_MODEL), 1.0)
    mem = nrm((BATCH, N_MEM, D_MODEL), 1.0)
    offset = jax.random.randint(next(ks), (BATCH, 1), 0, SEQ, dtype=jnp.int32)
    positions = offset + jnp.arange(SEQ, dtype=jnp.int32)[None, :]
    return {
        'x': x,
        'mem': mem,
        'positions': positions,
        'ffn1_norm': gain((DEPTH_2, D_MODEL)),
        'ffn1_w_gate': nrm((DEPTH_2, D_MODEL, D_FF_2), D_MODEL ** -0.5),
        'ffn1_w_up': nrm((DEPTH_2, D_MODEL, D_FF_2), D_MODEL ** -0.5),
        'ffn1_w_down': nrm((DEPTH_2, D_FF_2, D_MODEL), D_FF_2 ** -0.5),
        'mix_norm': gain((DEPTH_2, D_MODEL)),
        'mem_norm': gain((DEPTH_2, D_MODEL)),
        'w_in': nrm((DEPTH_2, D_MODEL, IN_WIDTH_2), D_MODEL ** -0.5),
        'w_mem_kv': nrm((DEPTH_2, D_MODEL, 2 * MEM_WIDTH), D_MODEL ** -0.5),
        'mem_q_norm': gain((DEPTH_2, HEAD_DIM)),
        'mem_k_norm': gain((DEPTH_2, HEAD_DIM)),
        'w_out': nrm((DEPTH_2, SELF_WIDTH + MEM_WIDTH, D_MODEL), (SELF_WIDTH + MEM_WIDTH) ** -0.5),
        'a_q_norm': gain((N_A_LAYERS, HEAD_DIM)),
        'a_k_norm': gain((N_A_LAYERS, HEAD_DIM)),
        'a_rel_bias': nrm((N_A_LAYERS, N_SELF_HEADS, N_REL), 0.1),
        'b_q_norm': gain((N_B_LAYERS, HEAD_DIM)),
        'b_k_norm': gain((N_B_LAYERS, HEAD_DIM)),
        'b_lambda_q1': nrm((N_B_LAYERS, HEAD_DIM), 0.1),
        'b_lambda_k1': nrm((N_B_LAYERS, HEAD_DIM), 0.1),
        'b_lambda_q2': nrm((N_B_LAYERS, HEAD_DIM), 0.1),
        'b_lambda_k2': nrm((N_B_LAYERS, HEAD_DIM), 0.1),
        'b_subln': gain((N_B_LAYERS, 2 * HEAD_DIM)),
        'ffn2_norm': gain((DEPTH_2, D_MODEL)),
        'ffn2_w_gate': nrm((DEPTH_2, D_MODEL, D_FF_2), D_MODEL ** -0.5),
        'ffn2_w_up': nrm((DEPTH_2, D_MODEL, D_FF_2), D_MODEL ** -0.5),
        'ffn2_w_down': nrm((DEPTH_2, D_FF_2, D_MODEL), D_FF_2 ** -0.5),
    }

def second_block(x, mem, positions, ffn1_norm, ffn1_w_gate, ffn1_w_up, ffn1_w_down,
              mix_norm, mem_norm, w_in, w_mem_kv, mem_q_norm, mem_k_norm, w_out,
              a_q_norm, a_k_norm, a_rel_bias, b_q_norm, b_k_norm,
              b_lambda_q1, b_lambda_k1, b_lambda_q2, b_lambda_k2, b_subln,
              ffn2_norm, ffn2_w_gate, ffn2_w_up, ffn2_w_down):
    B, S, _ = x.shape
    cos, sin = rope_tables(positions)
    cos = cos[:, :, None, None, :]
    sin = sin[:, :, None, None, :]

    for i in range(DEPTH_2):
        h = rmsnorm(x, ffn1_norm[i])
        x = x + 0.5 * swiglu(h, ffn1_w_gate[i], ffn1_w_up[i], ffn1_w_down[i])

        h = rmsnorm(x, mix_norm[i])
        proj = h @ w_in[i]
        q_s, k_s, v_s, q_m = jnp.split(proj, [SELF_WIDTH, 2 * SELF_WIDTH, 3 * SELF_WIDTH], axis=-1)

        mkv = rmsnorm(mem, mem_norm[i]) @ w_mem_kv[i]
        k_m, v_m = jnp.split(mkv, 2, axis=-1)
        q_m = rmsnorm(q_m.reshape(B, S, N_MEM_HEADS, HEAD_DIM), mem_q_norm[i])
        k_m = rmsnorm(k_m.reshape(B, N_MEM, N_MEM_HEADS, HEAD_DIM), mem_k_norm[i])
        v_m = v_m.reshape(B, N_MEM, N_MEM_HEADS, HEAD_DIM)
        o_m = memory_attention(q_m, k_m, v_m).reshape(B, S, MEM_WIDTH)

        j = i // N_MIXERS
        if i % N_MIXERS == 0:
            q = rmsnorm(q_s.reshape(B, S, N_SELF_HEADS, HEAD_DIM), a_q_norm[j])
            k = rmsnorm(k_s.reshape(B, S, N_SELF_HEADS, HEAD_DIM), a_k_norm[j])
            v = v_s.reshape(B, S, N_SELF_HEADS, HEAD_DIM)
            o_s = chunked_rel_attention(q, k, v, a_rel_bias[j]).reshape(B, S, SELF_WIDTH)
        else:
            lambda_init = 0.8 - 0.6 * math.exp(-0.3 * i)
            q = rmsnorm(q_s.reshape(B, S, N_DIFF_HEADS, 2, HEAD_DIM), b_q_norm[j])
            k = rmsnorm(k_s.reshape(B, S, N_DIFF_HEADS, 2, HEAD_DIM), b_k_norm[j])
            q = apply_rope(q, cos, sin)
            k = apply_rope(k, cos, sin)
            v = v_s.reshape(B, S, N_DIFF_HEADS, 2 * HEAD_DIM)
            lam = (jnp.exp(jnp.sum(b_lambda_q1[j].astype(jnp.float32) * b_lambda_k1[j].astype(jnp.float32)))
                   - jnp.exp(jnp.sum(b_lambda_q2[j].astype(jnp.float32) * b_lambda_k2[j].astype(jnp.float32)))
                   + lambda_init)
            o = diff_attention(q, k, v, lam)
            o = rmsnorm(o, b_subln[j]) * (1.0 - lambda_init)
            o_s = o.reshape(B, S, SELF_WIDTH)

        x = x + jnp.concatenate([o_s, o_m], axis=-1) @ w_out[i]

        h = rmsnorm(x, ffn2_norm[i])
        x = x + 0.5 * swiglu(h, ffn2_w_gate[i], ffn2_w_up[i], ffn2_w_down[i])
    return x


def setup_inputs(seed=0):
    out = dict(first_inputs(seed))
    for name, value in second_inputs(seed + 1).items():
        if name != "x":
            out[name + "_2"] = value
    return out


def reference(
    x, norm_mix_g, w_in, conv_w, b_igate, b_fgate, mlstm_norm_g, w_proj_a, w_proj_b, w_out,
    norm_ffn_g, w_gate_up, w_down, norm_final_g, mem_2, positions_2, ffn1_norm_2, ffn1_w_gate_2,
    ffn1_w_up_2, ffn1_w_down_2, mix_norm_2, mem_norm_2, w_in_2, w_mem_kv_2, mem_q_norm_2,
    mem_k_norm_2, w_out_2, a_q_norm_2, a_k_norm_2, a_rel_bias_2, b_q_norm_2, b_k_norm_2,
    b_lambda_q1_2, b_lambda_k1_2, b_lambda_q2_2, b_lambda_k2_2, b_subln_2, ffn2_norm_2,
    ffn2_w_gate_2, ffn2_w_up_2, ffn2_w_down_2,
):
    x = first_block(
        x, norm_mix_g, w_in, conv_w, b_igate, b_fgate, mlstm_norm_g, w_proj_a, w_proj_b, w_out,
        norm_ffn_g, w_gate_up, w_down, norm_final_g,
    )
    return second_block(
        x, mem_2, positions_2, ffn1_norm_2, ffn1_w_gate_2, ffn1_w_up_2, ffn1_w_down_2,
        mix_norm_2, mem_norm_2, w_in_2, w_mem_kv_2, mem_q_norm_2, mem_k_norm_2, w_out_2,
        a_q_norm_2, a_k_norm_2, a_rel_bias_2, b_q_norm_2, b_k_norm_2, b_lambda_q1_2,
        b_lambda_k1_2, b_lambda_q2_2, b_lambda_k2_2, b_subln_2, ffn2_norm_2, ffn2_w_gate_2,
        ffn2_w_up_2, ffn2_w_down_2,
    )


_drawn_inputs = setup_inputs


def setup_inputs(seed=0):
    import zlib

    import numpy as np

    out = dict(_drawn_inputs(seed))
    spreads = {}
    factors = {'norm_mix_g': 3.149,
     'b_igate': 64.0,
     'mlstm_norm_g': 6.111,
     'norm_ffn_g': 3.304,
     'ffn1_norm_2': 4.41,
     'mix_norm_2': 3.773,
     'mem_norm_2': 8.0,
     'mem_q_norm_2': 8.0,
     'mem_k_norm_2': 8.0,
     'a_q_norm_2': 8.0,
     'a_k_norm_2': 8.0,
     'a_rel_bias_2': 4.225,
     'b_q_norm_2': 8.0,
     'b_k_norm_2': 7.133,
     'b_lambda_k1_2': 5.093,
     'b_lambda_k2_2': 5.672,
     'b_subln_2': 51.632,
     'ffn2_norm_2': 5.145}
    for name, (base, spread) in spreads.items():
        noise = np.random.default_rng([zlib.crc32(name.encode()), seed]).standard_normal(out[name].shape)
        drawn = base * np.exp(spread * noise) if base else spread * noise
        out[name] = __import__('jax').numpy.asarray(drawn.astype(out[name].dtype))
    for name, factor in factors.items():
        out[name] = (out[name] * factor).astype(out[name].dtype)
    return out
```

```python
import math
from contextlib import ExitStack

import numpy as np

import concourse.bass as bass
from concourse import mybir

F32 = mybir.dt.float32
F32R = mybir.dt.float32r
I32 = mybir.dt.int32
ACT = mybir.ActivationFunctionType
ALU = mybir.AluOpType
AX_X = mybir.AxisListType.X

P = 128
SEQ = 256
DM = 1024
RT = SEQ // P
KC = DM // P
EPS = 1e-6
MASKED = -1e30

AH, AD = 8, 64
BH, BD = 4, 128
CONV = 4
FF = 2816
SH, MH, HD = 12, 4, 64
DH = SH // 2
SW, MW = SH * HD, MH * HD
ZW = 3 * SW + MW
N_REL, REL_CLIP = 257, 128
LAM_INIT = 0.8 - 0.6 * math.exp(-0.3)
SCALE = HD ** -0.5

UW = 2048
STEPS = FF // 256
FF_UNITS = 3 * STEPS
QA, KA, VA, QKB, VB, OB, GA, GB = 0, 2, 4, 6, 10, 12, 14, 18
PROJ = 22
WO = [26, 108, 190]
FFU = [30, 65, 112, 147, 194]
MEMU = [63, 145]
MIXU = [98, 180]
N_UNITS = FFU[4] + FF_UNITS
assert WO[0] + 4 == FFU[0] and FFU[0] + FF_UNITS == MEMU[0] and MEMU[0] + 2 == FFU[1]
assert FFU[1] + FF_UNITS == MIXU[0] and MIXU[0] + 10 == WO[1] and WO[1] + 4 == FFU[2]
assert FFU[2] + FF_UNITS == MEMU[1] and FFU[3] + FF_UNITS == MIXU[1] and WO[2] + 4 == FFU[4]

N_MIX, N_FFN, N_MEM0, N_FIN, N_F1, N_M0, N_F2, N_MEM1, N_F3, N_M1, N_F4 = range(11)
T_MIX, T_Y0, T_FFN, T_MEM0, T_F1, T_M0, T_Y1, T_F2, T_MEM1, T_F3, T_M1, T_Y2, T_F4 = range(13)
R_WO0, R_FF0, R_F1, R_WO1, R_F2, R_F3, R_WO2, R_F4 = range(8)

ITEMS = [("A", rt, a, -1) for rt in range(RT) for a in range(AH // 2)]
ITEMS += [("M", rt, a, -1) for rt in range(RT) for a in range(BH // 2)]
for _layer, _kind in enumerate("RD"):
    for _rt in range(RT):
        ITEMS += [(_kind, _rt, a, _layer) for a in range(SH // 2)]
        ITEMS += [("X", _rt, a, _layer) for a in range(MH // 2)]
IT0 = [12, 28]
N_IT = 16
SOFT = np.cumsum([k != "M" for k, *_ in ITEMS]).tolist()
DIFF = np.cumsum([k == "D" for k, *_ in ITEMS]).tolist()
STREAM0 = {"b1": 0, "mem0": 22, "mix0": 24, "mem1": 34, "mix1": 36}

C_ID, C_MA, C_TRI, C_ONE, C_COS, C_SIN, C_MB, C_INV = 0, 128, 384, 512, 640, 768, 896, 1152
C_W = 1184


def shape_constants():
    c = np.zeros((P, C_W), np.float32)
    i = np.arange(P)
    c[:, C_ID:C_ID + P] = np.eye(P)
    c[:, C_MA + P:C_MA + 2 * P] = np.where(i[None, :] > i[:, None], MASKED, 0.0)
    c[:, C_TRI:C_TRI + P] = i[:, None] <= i[None, :]
    c[:, C_ONE:C_ONE + P] = 1.0
    half = AD // 2
    inv = np.float32(10000.0) ** (-np.arange(half, dtype=np.float32) / np.float32(half))
    for rt in range(RT):
        ang = ((rt * P + i).astype(np.float32)[:, None] * inv[None, :]).astype(np.float64)
        c[:, C_COS + rt * AD:C_COS + rt * AD + AD] = np.concatenate([np.cos(ang)] * 2, 1)
        c[:, C_SIN + rt * AD:C_SIN + rt * AD + AD] = np.concatenate([-np.sin(ang), np.sin(ang)], 1)
    c[0:64, C_MB + P + 64:C_MB + 2 * P] = MASKED
    c[:, C_INV:C_INV + 32] = np.float32(1.0) / (
        np.float32(10000.0) ** (np.arange(0, HD, 2, dtype=np.float32) / np.float32(HD)))
    return c


def build(nc, t, out):
    TWO_PI = 2 * math.pi
    PI_1 = 6.28125
    PI_2 = math.floor((TWO_PI - PI_1) * 2 ** 21) / 2 ** 21
    PI_3 = TWO_PI - PI_1 - PI_2
    ROUND = 12582912.0
    PI_LIM = 3.1415925

    with ExitStack() as ctx:
        def sb(name, shape, dt=F32):
            return ctx.enter_context(nc.sbuf_tensor(name, shape, dt))

        def sem(name):
            return ctx.enter_context(nc.semaphore(name))

        raw = sb("raw", [P, 3, UW])
        whi = sb("whi", [P, 3, UW], F32R)
        wlo = sb("wlo", [P, 3, UW], F32R)
        xhi = sb("xhi", [P, KC, SEQ], F32R)
        xlo = sb("xlo", [P, KC, SEQ], F32R)
        hhi = sb("hhi", [P, 2, 512], F32R)
        hlo = sb("hlo", [P, 2, 512], F32R)
        res = sb("res", [P, RT, DM])
        xn = sb("xn", [P, RT, DM])
        gain = sb("gain", [P, 2, DM])
        work = sb("work", [P, 14848])
        sc = sb("sc", [P, 2, 512])
        pr = sb("pr", [P, 2, 512])
        pT = sb("pT", [P, 2, 512])
        sq = sb("sq", [P, 2, 512])
        cst = sb("cst", [P, C_W])
        wif = sb("wif", [P, KC, 2 * BH])
        wifh = sb("wifh", [P, KC, 2 * BH], F32R)
        wifl = sb("wifl", [P, KC, 2 * BH], F32R)
        bif = sb("bif", [P, 2 * BH])
        cwr = sb("cwr", [32, P])
        cw = sb("cw", [P, 32])
        gml = sb("gml", [P, BH * BD])
        colg = sb("colg", [P, 8])
        headg = sb("headg", [P, 2, HD])
        lam = sb("lam", [P, 8])
        gsub = sb("gsub", [P, 2 * HD])
        posi = sb("posi", [P, RT], I32)
        posf = sb("posf", [P, RT])
        ropeq = sb("ropeq", [P, 2, RT, HD])
        ropek = sb("ropek", [P, 2, RT, HD])
        small = sb("small", [P, 160])
        ss = sb("ss", [P, 22])
        ms = sb("ms", [P, 22])
        rstd = sb("rstd", [P, 22])
        hss = sb("hss", [P, 4, 8])
        hms = sb("hms", [P, 4, 8])
        hrs = sb("hrs", [P, 4, 8])
        mhalf = sb("mhalf", [P, 1])
        sums = sb("sums", [P, 2 * len(ITEMS)])
        nmax = sb("nmax", [P, 2 * len(ITEMS)])
        rec = sb("rec", [P, 48])
        cf = sb("cf", [P, 4])

        ps = ctx.enter_context(nc.psum_tensor("ps", [P, 8, 512], F32))
        relx = nc.dram_tensor("relx", [SH, 512], F32).ap()

        def region(off, *shape):
            n = int(np.prod(shape))
            v = work[:, off:off + n]
            if len(shape) == 2:
                v = v.rearrange("p (a b) -> p a b", b=shape[1])
            if len(shape) == 3:
                v = v.rearrange("p (a b c) -> p a b c", b=shape[1], c=shape[2])
            return v

        z1 = region(0, RT, 5, 512)
        qkb = region(5120, 2 * BH, SEQ)
        sga = region(7168, KC, SEQ)
        sgb = region(9216, KC, SEQ)
        cin = region(9216, 2 * BH, SEQ)
        relr = region(7168, N_REL)
        rele = region(7168 + 260, 512)
        qT = region(11264, 4, SEQ)
        kT = region(12288, 4, SEQ)
        diag = region(11264, RT, BH, P)
        trig = region(7960, 7, 64)
        lamv = region(8408, 4, HD)
        lw = region(13312, BH, 384)
        z2 = region(0, RT, ZW)
        memx = region(0, RT, DM)
        qkT = region(5120, 12, SEQ)
        qmT = region(8192, 2, SEQ)
        kmT = region(8704, 2, SEQ)
        kv = region(9216, RT, 512)
        toep = region(10240, SH, SEQ)
        rt1 = region(10240, 512)
        rt2 = region(10752, 512)
        comb = region(13312, 2, SEQ)
        sil = pr[:, 0, :]
        hid = sc[:, 0, :]

        ident = cst[:, C_ID:C_ID + P]

        const_full, cst_full, wif_full = sem("const_full"), sem("cst_full"), sem("wif_full")
        x_full = [sem(f"x_full{r}") for r in range(RT)]
        raw_full = [sem(f"raw_full{s}") for s in range(3)]
        gain_full = [sem(f"gain_full{s}") for s in range(2)]
        mem_full, toep_full, rel_full, relx_full = sem("mem_full"), sem("toep_full"), sem("rel_full"), sem("relx_full")
        out_full = sem("out_full")
        hi_done, lo_done, unit_used = sem("hi_done"), sem("lo_done"), sem("unit_used")
        sq_done, rstd_ready, xn_ready, pool_ms = sem("sq_done"), sem("rstd_ready"), sem("xn_ready"), sem("pool_ms")
        tr_ps, xhi_done, xlo_done = sem("tr_ps"), sem("xhi_done"), sem("xlo_done")
        acc0_ready, res_done = sem("acc0_ready"), sem("res_done")
        silu_done, h_mul, h_hi, h_ready = sem("silu_done"), sem("h_mul"), sem("h_hi"), sem("h_ready")
        stream_evac = sem("stream_evac")
        wif_hi, wif_lo = sem("wif_hi"), sem("wif_lo")
        gate_ps, gate_act, gate_dve = sem("gate_ps"), sem("gate_act"), sem("gate_dve")
        lw_exp = sem("lw_exp")
        dve_chain, act_chain, pool_chain = sem("dve_chain"), sem("act_chain"), sem("pool_chain")
        rope_ready, qk_ps, qk_sb = sem("rope_ready"), sem("qk_ps"), sem("qk_sb")
        conv_ready, qkb_ready, ob_ready = sem("conv_ready"), sem("qkb_ready"), sem("ob_ready")
        sc_ready, sc_read, p_ready, comb_ready = sem("sc_ready"), sem("sc_read"), sem("p_ready"), sem("comb_ready")
        pT_ready, pT_evac, pv_ready, o_evac = sem("pT_ready"), sem("pT_evac"), sem("pv_ready"), sem("o_evac")
        mh_ready, hsq_ready, hss_ready, hms_done, hrs_ready = (
            sem("mh_ready"), sem("hsq_ready"), sem("hss_ready"), sem("hms_done"), sem("hrs_ready"))
        zn_ready, y_ready = sem("zn_ready"), sem("y_ready")
        merged_sum, merged_hi, merged_lo = sem("merged_sum"), sem("merged_hi"), sem("merged_lo")
        toep_ready, trig_in, trig_out, lam_in, lam_out = (
            sem("toep_ready"), sem("trig_in"), sem("trig_out"), sem("lam_in"), sem("lam_out"))
        ext_ready, bias_full = sem("ext_ready"), sem("bias_full")
        tr_heads, heads_sb = sem("tr_heads"), sem("heads_sb")
        N_CONST = 21

        block = ctx.enter_context(nc.Block())

        @block.sync
        def _(sp):
            def fill(u, slot, src, a):
                if not isinstance(u, int) or u >= 3:
                    sp.wait_ge(lo_done, u - 2)
                sp.dma_start(raw[:, slot, :].rearrange("p (a b) -> p a b", a=a), src)\
                    .then_inc(raw_full[slot], 16)

            def cols(w, k0, nk, c0, n):
                return w.rearrange("(k p) n -> p k n", p=P)[:, k0:k0 + nk, bass.ds(c0, n)]

            def rows(w, k0):
                return w.rearrange("(j c p) n -> p j (c n)", p=P, c=2)[:, bass.ds(k0, 1), :]

            def down(w, j):
                return w.rearrange("(j c p) n -> p j c n", p=P, c=2)[:, bass.ds(j, 1), :, :]\
                    .rearrange("p j c n -> p (j c) n")

            def wide(u, w, c0):
                for k in range(2):
                    fill(u + k, (u + k) % 3, cols(w, 4 * k, 4, c0, 512), 4)

            def ffn(u0, gate, g0, up, p0, dn):
                def gate_up(u, slot, j):
                    fill(u, slot, cols(gate, 0, KC, g0 + 256 * j, 256), KC)
                    fill(u + 1, (slot + 1) % 3, cols(up, 0, KC, p0 + 256 * j, 256), KC)
                gate_up(u0, u0 % 3, 0)
                gate_up(u0 + 2, (u0 + 2) % 3, 1)
                fill(u0 + 4, (u0 + 4) % 3, down(dn, 0), 2)
                with sp.Fori(0, (STEPS - 3) // 2) as i:
                    for k in range(2):
                        u = u0 + 5 + 3 * k
                        gate_up(i * 6 + u, u % 3, i * 2 + (2 + k))
                        fill(i * 6 + (u + 2), (u + 2) % 3, down(dn, i * 2 + (1 + k)), 2)
                gate_up(u0 + 29, (u0 + 29) % 3, STEPS - 1)
                for j in (STEPS - 2, STEPS - 1):
                    u = u0 + 31 + j - (STEPS - 2)
                    fill(u, u % 3, down(dn, j), 2)

            for r in range(RT):
                sp.dma_start(res[:, r, :], t["x"][0, r * P:(r + 1) * P, :]).then_inc(x_full[r], 16)
            w_in = t["w_in"][0]
            wide(QA, w_in, 0)
            wide(KA, w_in, 512)
            wide(VA, w_in, 1024)
            for n in range(4):
                fill(QKB + n, (QKB + n) % 3, cols(w_in, 0, KC, 1536 + 256 * n, 256), KC)
            wide(VB, w_in, 2560)
            wide(OB, w_in, 3072)
            for n in range(8):
                fill(GA + n, (GA + n) % 3, cols(w_in, 0, KC, 3592 + 256 * n, 256), KC)
            for m in range(4):
                w = t["w_proj_b" if m % 2 else "w_proj_a"][0]
                fill(PROJ + m, (PROJ + m) % 3, cols(w, 0, 4, 512 * (m // 2), 512), 4)
            for m in range(4):
                fill(WO[0] + m, (WO[0] + m) % 3, down(t["w_out"][0], m), 2)
            gu = t["w_gate_up"][0]
            ffn(FFU[0], gu, 0, gu, FF, t["w_down"][0])
            for L in range(2):
                wide(MEMU[L], t["w_mem_kv_2"][L], 0)
                ffn(FFU[1 + 2 * L], t["ffn1_w_gate_2"][L], 0, t["ffn1_w_up_2"][L], 0, t["ffn1_w_down_2"][L])
                for s in range(5):
                    wide(MIXU[L] + 2 * s, t["w_in_2"][L], 512 * s)
                for m in range(4):
                    fill(WO[1 + L] + m, (WO[1 + L] + m) % 3, down(t["w_out_2"][L], m), 2)
                ffn(FFU[2 + 2 * L], t["ffn2_w_gate_2"][L], 0, t["ffn2_w_up_2"][L], 0, t["ffn2_w_down_2"][L])
            for r in range(RT):
                sp.wait_ge(res_done, 2 * R_F4 + r + 1)
                sp.dma_start(out[0, r * P:(r + 1) * P, :], res[:, r, :]).then_inc(out_full, 16)
            sp.wait_ge(out_full, 16 * RT)

        @block.gpsimd
        def _(pool):
            def load(dst, src):
                pool.dma_start(dst, src).then_inc(const_full, 16)

            def across(v):
                return bass.AP(tensor=v.tensor, offset=v.offset, ap=[[0, P]] + [list(x) for x in v.ap])

            norm_gain = [t["norm_mix_g"][0], t["norm_ffn_g"][0], t["mem_norm_2"][0], t["norm_final_g"],
                         t["ffn1_norm_2"][0], t["mix_norm_2"][0], t["ffn2_norm_2"][0], t["mem_norm_2"][1],
                         t["ffn1_norm_2"][1], t["mix_norm_2"][1], t["ffn2_norm_2"][1]]

            def load_gain(n):
                if n >= 2:
                    pool.wait_ge(xn_ready, 2 * (n - 1))
                pool.dma_start(gain[:, n % 2, :], across(norm_gain[n])).then_inc(gain_full[n % 2], 16)

            def norm(n):
                for r in range(RT):
                    c = 2 * n + r
                    pool.wait_ge(sq_done, c + 1)
                    pool.tensor_scalar(ms[:, c:c + 1], ss[:, c:c + 1], 1.0 / DM, EPS, ALU.mult, ALU.add)\
                        .then_inc(pool_ms, 1)
                    pool.wait_ge(pool_ms, c + 1)
                    pool.tensor_tensor(rstd[:, c:c + 1], ms[:, c:c + 1], mhalf[:, :], ALU.pow)\
                        .then_inc(rstd_ready, 1)

            def head_norm(e, n, size):
                pool.wait_ge(hss_ready, e + 1)
                pool.tensor_scalar(hms[:, e % 4, 0:n], hss[:, e % 4, 0:n], 1.0 / size, EPS, ALU.mult, ALU.add)\
                    .then_inc(hms_done, 1)
                pool.wait_ge(hms_done, e + 1)
                pool.tensor_tensor(hrs[:, e % 4, 0:n], hms[:, e % 4, 0:n], mhalf[:, :].to_broadcast([P, n]),
                                   ALU.pow).then_inc(hrs_ready, 1)

            pool.memset(mhalf[:, :], -0.5).then_inc(pool_chain, 1)
            load_gain(0)
            load_gain(1)
            pool.dma_start(bif[:, 0:BH], across(t["b_igate"][0])).then_inc(bias_full, 16)
            pool.dma_start(bif[:, BH:2 * BH], across(t["b_fgate"][0])).then_inc(bias_full, 16)
            pool.dma_start(cwr[:, :], t["conv_w"][0].rearrange("j (c p) -> (j c) p", p=P)).then_inc(bias_full, 16)
            load(gml[:, :], across(t["mlstm_norm_g"][0]))
            pool.wait_ge(pool_chain, 1)
            norm(N_MIX)
            with nc.allow_non_contiguous_dma(reason="small"):
                load(posi[:, :], t["positions_2"].rearrange("a (r p) -> p (a r)", p=P))
                col = [t["a_q_norm_2"][0], t["a_k_norm_2"][0], t["mem_q_norm_2"][0], t["mem_k_norm_2"][0],
                       t["mem_q_norm_2"][1], t["mem_k_norm_2"][1]]
                pool.dma_start(relr[0:SH, :], t["a_rel_bias_2"][0]).then_inc(rel_full, 16)
                for n, v in enumerate(col):
                    for half in range(2):
                        load(colg[HD * half:HD * half + HD, n:n + 1], v.rearrange("(p a) -> p a", a=1))
            for n, v in enumerate(["b_q_norm_2", "b_k_norm_2"]):
                load(headg[:, n, :], across(t[v][0]))
            for n, v in enumerate(["b_lambda_q1_2", "b_lambda_k1_2", "b_lambda_q2_2", "b_lambda_k2_2"]):
                load(lamv[:, n, :], across(t[v][0]))
            load(gsub[:, :], across(t["b_subln_2"][0]))

            pool.wait_ge(ext_ready, 2)
            pool.dma_start(relx, rele[0:SH, :]).then_inc(relx_full, 16)
            for e in range(2):
                head_norm(e, BH, BD)
            load_gain(2)
            norm(N_FFN)
            pool.wait_ge(merged_lo, 4)
            pool.dma_start(memx, t["mem_2"][0].rearrange("(r p) d -> p r d", p=P)).then_inc(mem_full, 16)
            pool.wait_ge(relx_full, 16)
            diagonals = bass.AP(tensor=relx.tensor, offset=0, ap=[[1, P], [512, SH], [1, SEQ]])
            pool.dma_start(toep, diagonals).then_inc(toep_full, 16)
            pool.wait_ge(toep_full, 16)
            pool.memset(toep[0:64, :, 0:64], MASKED).then_inc(toep_ready, 1)
            for L in range(2):
                n = N_MEM0 + 5 * L
                load_gain(n + 1)
                norm(n)
                if L == 0:
                    load_gain(N_F1)
                    norm(N_FIN)
                    load_gain(N_M0)
                    norm(N_F1)
                    load_gain(N_F2)
                else:
                    load_gain(N_M1)
                    norm(N_F3)
                    load_gain(N_F4)
                eb = 2 + 10 * L
                for e in range(2):
                    head_norm(eb + e, MH, HD)
                norm(N_M0 if L == 0 else N_M1)
                for e in range(2, 8):
                    head_norm(eb + e, 8, HD)
                for e in range(8, 10):
                    head_norm(eb + e, MH, HD)
                if L == 0:
                    load_gain(N_MEM1)
                    pool.wait_ge(y_ready, 4)
                    pool.dma_start(memx, t["mem_2"][0].rearrange("(r p) d -> p r d", p=P)).then_inc(mem_full, 16)
                    norm(N_F2)
                else:
                    for e in range(2):
                        head_norm(22 + e, DH, 2 * HD)
                    norm(N_F4)

        @block.scalar
        def _(act):
            def hi(u, slot):
                act.wait_ge(raw_full[slot], 16 * (u // 3 + 1))
                if u >= 3:
                    act.wait_ge(unit_used, u - 2)
                act.activation(whi[:, slot, :], raw[:, slot, :], ACT.Copy).then_inc(hi_done, 1)

            def hi_at(i, c):
                act.wait_ge(raw_full[c % 3], i * 32 + 16 * (c // 3 + 1))
                act.wait_ge(unit_used, i * 6 + (c - 2))
                act.activation(whi[:, c % 3, :], raw[:, c % 3, :], ACT.Copy).then_inc(hi_done, 1)

            def square(n, src, r, *waits):
                for s, v in waits:
                    act.wait_ge(s, v)
                c = 2 * n + r
                act.activation(xn[:, r, :], src[:, r, :], ACT.Square, accum_out=ss[:, c:c + 1]).then_inc(sq_done, 1)

            def turned(T):
                for b in range(4):
                    act.wait_ge(tr_ps, 4 * T + b + 1)
                    act.activation(xhi[:, 2 * b:2 * b + 2, :].rearrange("p a b -> p (a b)"), ps[:, b, :], ACT.Copy)\
                        .then_inc(xhi_done, 1)

            def head_square(e, src, n):
                if e >= 2:
                    act.wait_ge(hss_ready, e - 1)
                act.activation(sq[:, e % 2, 0:n], src, ACT.Square).then_inc(hsq_ready, 1)

            def exps(i):
                kind, r, a, L = ITEMS[i]
                nk = SEQ if kind == "X" else P * (r + 1)
                act.wait_ge(sc_read, i + 1)
                if i >= 2:
                    act.wait_ge(pT_ready, i - 1)
                for e in range(2):
                    src = ps[:, 2 * (i % 2) + e, 0:nk] if kind == "X" else sc[:, i % 2, 256 * e:256 * e + nk]
                    ins = act.activation(pr[:, i % 2, 256 * e:256 * e + nk], src, ACT.Exp,
                                         bias=nmax[:, 2 * i + e:2 * i + e + 1],
                                         scale=SCALE if kind == "X" else 1.0,
                                         accum_out=sums[:, 2 * i + e:2 * i + e + 1])
                ins.then_inc(p_ready, 1)

            def evac_pT(i):
                kind, r, a, L = ITEMS[i]
                n = (1 if kind == "D" else 2) * (2 if kind == "X" else r + 1) * P
                bank = 6 if L < 0 else 4 + i % 2
                act.wait_ge(pT_ready, i + 1)
                if i >= 2:
                    act.wait_ge(pv_ready, i - 1)
                act.activation(pT[:, i % 2, 0:n], ps[:, bank, 0:n], ACT.Copy).then_inc(pT_evac, 1)

            def ffn(f, u0, follow):
                j0 = STEPS * f

                def silu(J, u, bank):
                    act.wait_ge(unit_used, u)
                    if not isinstance(J, int) or J > 0:
                        act.wait_ge(h_mul, J)
                    act.activation(sil, ps[:, bank, :], ACT.Silu).then_inc(silu_done, 1)

                silu(j0, u0 + 1, 0)
                hi(u0 + 3, (u0 + 3) % 3)
                hi(u0 + 4, (u0 + 4) % 3)
                silu(j0 + 1, u0 + 3, 2)
                for c in range(u0 + 5, u0 + 8):
                    hi(c, c % 3)
                with act.Fori(0, (STEPS - 3) // 2) as i:
                    for k in range(2):
                        silu(i * 2 + (j0 + 2 + k), i * 6 + (u0 + 6 + 3 * k), 2 * k)
                        for c in range(u0 + 8 + 3 * k, u0 + 11 + 3 * k):
                            hi_at(i, c)
                silu(j0 + STEPS - 1, u0 + 30, 0)
                for c in range(u0 + 32, u0 + 32 + follow):
                    hi(c, c % 3)

            act.dma_start(cst[:, :], t["consts"]).then_inc(cst_full, 16)
            with nc.allow_non_contiguous_dma(reason="small"):
                act.dma_start(wif[:, :, :], t["w_in"][0].rearrange("(k p) n -> p k n", p=P)[:, :, 3584:3592])\
                    .then_inc(wif_full, 16)
            for r in range(RT):
                square(N_MIX, res, r, (x_full[r], 16))
            act.wait_ge(wif_full, 16)
            act.activation(wifh[:, :, :], wif[:, :, :], ACT.Copy).then_inc(wif_hi, 1)
            hi(0, 0)
            turned(T_MIX)
            hi(1, 1)
            hi(2, 2)

            def evac(n, dst, func=ACT.Copy):
                act.activation(dst, ps[:, n % 4, :], func).then_inc(stream_evac, 1)

            for u in range(PROJ):
                hi(u + 3, u % 3)
                if u == 0:
                    act.wait_ge(gate_dve, 2)
                    act.activation(small[:, 8:16], small[:, 0:8], ACT.Exp, scale=-1.0).then_inc(act_chain, 1)
                    act.wait_ge(act_chain, 1)
                    act.activation(small[:, 16:24], small[:, 8:16], ACT.Ln, bias=1.0).then_inc(gate_act, 1)
                act.wait_ge(unit_used, u + 1)
                if u in (QA + 1, KA + 1, VA + 1, VB + 1, OB + 1):
                    s = {QA: 0, KA: 1, VA: 2, VB: 3, OB: 4}[u - 1]
                    n0 = {0: 0, 1: 2, 2: 4, 3: 10, 4: 12}[s]
                    for r in range(RT):
                        evac(n0 + r, z1[:, r, s, :])
                if QKB <= u < VB:
                    j = u - QKB
                    evac(6 + j, cin[:, 2 * j:2 * j + 2, :].rearrange("p a b -> p (a b)"))
                if u == 2:
                    act.wait_ge(gate_dve, 7)
                    for r in range(RT):
                        for h in range(BH):
                            v = lw[:, h, 0:P] if r == 0 else lw[:, h, P:3 * P]
                            act.activation(v, v, ACT.Exp, bias=small[:, 40 + 4 * r + h:41 + 4 * r + h])
                    act.activation(small[:, 56:64], small[:, 48:56], ACT.Exp, scale=-1.0).then_inc(lw_exp, 1)
                if u in (5, 6):
                    for b in range(2):
                        n = 2 * (u - 5) + b
                        act.wait_ge(qk_ps, n + 1)
                        dst = (qT, kT)[u - 5][:, 2 * b:2 * b + 2, :].rearrange("p a b -> p (a b)")
                        act.activation(dst, ps[:, 4 + n, :], ACT.Copy).then_inc(qk_sb, 1)
                if u >= 7:
                    k = u - 7
                    if 1 <= k <= 12:
                        evac_pT(k - 1)
                    if k < 8:
                        exps(k)
                if u == 5:
                    act.wait_ge(lam_in, 2)
                    act.activation(lam[:, 2:4], lam[:, 0:2], ACT.Exp).then_inc(lam_out, 1)
                    act.wait_ge(trig_in, 2)
                    act.activation(trig[:, 5:7, :], trig[:, 3:5, :], ACT.Sin).then_inc(trig_out, 1)
                if u == 14:
                    act.wait_ge(conv_ready, 8)
                    act.activation(qkb, qkb, ACT.Silu).then_inc(qkb_ready, 1)
                    act.activation(z1[:, :, 4, :], z1[:, :, 4, :], ACT.Sigmoid).then_inc(ob_ready, 1)
                if GA <= u < PROJ:
                    j = u - GA
                    if j == 0:
                        act.wait_ge(relx_full, 16)
                    dst = (sga, sgb)[j // 4][:, 2 * (j % 4):2 * (j % 4) + 2, :].rearrange("p a b -> p (a b)")
                    evac(14 + j, dst, ACT.Sigmoid)
                if u in (18, 20):
                    r = (u - 18) // 2
                    act.wait_ge(mh_ready, r + 1)
                    head_square(r, xn[:, r, 512:1024], 512)
            turned(T_Y0)
            for m in range(2):
                hi(PROJ + 3 + 2 * m, (PROJ + 3 + 2 * m) % 3)
                hi(PROJ + 4 + 2 * m, (PROJ + 4 + 2 * m) % 3)
                for b in range(2 * m, 2 * m + 2):
                    act.wait_ge(merged_sum, b + 1)
                    dst = hhi[:, b, :] if b < 2 else xhi[:, 2 * b:2 * b + 2, :].rearrange("p a b -> p (a b)")
                    act.activation(dst, sc[:, b % 2, :], ACT.Copy).then_inc(merged_hi, 1)

            def out_stream(w):
                for m in range(4):
                    hi(w + 3 + m, (w + 3 + m) % 3)

            out_stream(WO[0])
            for r in range(RT):
                square(N_FFN, res, r, (res_done, 2 * R_WO0 + r + 1))
            turned(T_FFN)

            act.wait_ge(const_full, 16 * N_CONST)
            for r in range(RT):
                square(N_MEM0, memx, r, (mem_full, 16))
            ffn(0, FFU[0], 3)
            turned(T_MEM0)
            for r in range(RT):
                square(N_FIN, res, r, (res_done, 2 * R_FF0 + r + 1))
            for r in range(RT):
                square(N_F1, res, r, (xn_ready, 2 * N_FIN + r + 1))

            def memory_rows(L):
                u = MEMU[L]
                hi(u + 2, (u + 2) % 3)
                hi(u + 3, u % 3)
                act.wait_ge(unit_used, u + 2)
                hi(u + 4, (u + 1) % 3)
                for r in range(RT):
                    head_square(2 + 10 * L + r, ps[:, 2 + r, 0:MW], MW)
                    act.activation(kv[:, r, :], ps[:, 2 + r, :], ACT.Copy).then_inc(stream_evac, 1)

            for L in range(2):
                memory_rows(L)
                turned(T_F1 + 5 * L)
                ffn(1 + 2 * L, FFU[1 + 2 * L], 3)
                u = MIXU[L]
                for r in range(RT):
                    square(N_M0 + 4 * L, res, r, (res_done, 2 * (R_F1 + 3 * L) + r + 1))
                hi(u + 2, (u + 2) % 3)
                turned(T_M0 + 5 * L)
                eb, tb, sb0 = 2 + 10 * L, 8 * L, STREAM0[f"mix{L}"]

                def heads(tt, dst, g):
                    act.wait_ge(tr_heads, tb + tt + 1)
                    dst = dst.rearrange("p a b -> p (a b)")
                    act.activation(dst, ps[:, 4 + tt % 4, :], ACT.Copy,
                                   scale=1.0 if g is None else colg[:, g:g + 1]).then_inc(heads_sb, 1)

                for m in range(10):
                    hi(u + m + 3, (u + m) % 3)
                    s = m // 2
                    if m % 2:
                        act.wait_ge(unit_used, u + m + 1)
                        for r in range(RT):
                            bank = (2 * s + r) % 4
                            if s < 3:
                                head_square(eb + 2 + 2 * s + r, ps[:, bank, :], 512)
                            if s == 4:
                                head_square(eb + 8 + r, ps[:, bank, 256:512], MW)
                            act.activation(z2[:, r, 512 * s:512 * s + 512], ps[:, bank, :], ACT.Copy)\
                                .then_inc(stream_evac, 1)
                        if s == 0:
                            heads(0, kmT, 3 + 2 * L)
                        if 1 <= s <= 3:
                            for b in range(2):
                                c = 2 * (2 * (s - 1) + b)
                                g = (0 if c < 6 else 1) if L == 0 else None
                                heads(1 + 2 * (s - 1) + b, qkT[:, c:c + 2, :], g)
                heads(7, qmT, 2 + 2 * L)
                i0 = IT0[L]
                for k in range(N_IT + 3):
                    if 2 <= k < N_IT + 2:
                        evac_pT(i0 + k - 2)
                    if k < N_IT:
                        exps(i0 + k)
                    if L == 1 and k in (10, 18):
                        r = (k - 10) // 8
                        act.wait_ge(pv_ready, i0 + 8 * (r + 1))
                        act.wait_ge(hss_ready, 22 + r)
                        act.activation(sq[:, :, :].rearrange("p a b -> p (a b)")[:, 0:SW],
                                       ps[:, 6:8, :].rearrange("p a b -> p (a b)")[:, 0:SW],
                                       ACT.Square).then_inc(hsq_ready, 1)
                turned(T_Y1 + 5 * L)
                out_stream(WO[1 + L])
                for r in range(RT):
                    square(N_F2 + 4 * L, res, r, (res_done, 2 * (R_WO1 + 3 * L) + r + 1))
                turned(T_F2 + 5 * L)
                if L == 0:
                    for r in range(RT):
                        square(N_MEM1, memx, r, (mem_full, 32))
                    ffn(2, FFU[2], 3)
                    turned(T_MEM1)
                    for r in range(RT):
                        square(N_F3, res, r, (res_done, 2 * R_F2 + r + 1))
                else:
                    ffn(4, FFU[4], 1)

        @block.vector
        def _(dve):
            count = [0]

            def link(ins):
                count[0] += 1
                ins.then_inc(dve_chain, 1)
                dve.wait_ge(dve_chain, count[0])

            def lo(u):
                dve.wait_ge(hi_done, u + 1)
                dve.tensor_tensor(wlo[:, u % 3, :], raw[:, u % 3, :], whi[:, u % 3, :], ALU.subtract)\
                    .then_inc(lo_done, 1)

            def lo_at(i, c):
                dve.wait_ge(hi_done, i * 6 + (c + 1))
                dve.tensor_tensor(wlo[:, c % 3, :], raw[:, c % 3, :], whi[:, c % 3, :], ALU.subtract)\
                    .then_inc(lo_done, 1)

            def scaled(n, src, dst, r):
                c = 2 * n + r
                dve.wait_ge(rstd_ready, c + 1)
                if r == 0:
                    dve.wait_ge(gain_full[n % 2], 16 * (n // 2 + 1))
                dve.scalar_tensor_tensor(out=dst[:, r, :], in0=src[:, r, :], scalar=rstd[:, c:c + 1],
                                         in1=gain[:, n % 2, :], op0=ALU.mult, op1=ALU.mult).then_inc(xn_ready, 1)

            def turned(T):
                for b in range(4):
                    dve.wait_ge(xhi_done, 4 * T + b + 1)
                    v = slice(2 * b, 2 * b + 2)
                    dve.tensor_tensor(xlo[:, v, :].rearrange("p a b -> p (a b)"), ps[:, b, :],
                                      xhi[:, v, :].rearrange("p a b -> p (a b)"), ALU.subtract)\
                        .then_inc(xlo_done, 1)

            def head_sum(e, n, size, width=None):
                dve.wait_ge(hsq_ready, e + 1)
                src = sq[:, e % 2, 0:n * size] if width is None else sq[:, :, :].rearrange("p a b -> p (a b)")[:, 0:width]
                dve.tensor_reduce(hss[:, e % 4, 0:n], src.rearrange("p (h d) -> p h d", d=size), AX_X, ALU.add)\
                    .then_inc(hss_ready, 1)

            def head_rstd(e, n, size):
                dve.wait_ge(hrs_ready, e + 1)
                return hrs[:, e % 4, 0:n].unsqueeze(2).to_broadcast([P, n, size])

            def residual(idx, u_last, factor, banks=(4, 6)):
                for r in range(RT):
                    if r == 0:
                        dve.wait_ge(acc0_ready, idx + 1)
                    else:
                        dve.wait_ge(unit_used, u_last + 1)
                    b = banks[r]
                    dve.scalar_tensor_tensor(out=res[:, r, :], in0=ps[:, b:b + 2, :].rearrange("p a b -> p (a b)"),
                                             scalar=factor, in1=res[:, r, :], op0=ALU.mult, op1=ALU.add)\
                        .then_inc(res_done, 1)

            def rotate(v, h, cos, sin, t1, t2):
                n = h * HD
                v3 = v.rearrange("p (h d) -> p h d", d=HD)
                swapped = v.rearrange("p (h two d) -> p h two d", two=2, d=HD // 2)[:, :, ::-1, :]
                s4 = sin.rearrange("p (two d) -> p two d", two=2).unsqueeze(1).to_broadcast([P, h, 2, HD // 2])
                dve.tensor_tensor(t1[:, 0:n].rearrange("p (h d) -> p h d", d=HD), v3,
                                  cos.unsqueeze(1).to_broadcast([P, h, HD]), ALU.mult)
                link(dve.tensor_tensor(t2[:, 0:n].rearrange("p (h two d) -> p h two d", two=2, d=HD // 2),
                                       swapped, s4, ALU.mult))
                return dve.tensor_tensor(v, t1[:, 0:n], t2[:, 0:n], ALU.add)

            def scores(i):
                kind, r, a, L = ITEMS[i]
                nk = SEQ if kind == "X" else P * (r + 1)
                bank = 4 if L < 0 else 2 * (i % 2)
                s = ps[:, bank:bank + 2, 0:nk]
                col = slice(2 * i, 2 * i + 2)
                dve.wait_ge(sc_ready, i + 1)
                if kind == "M":
                    off = P if r else 0
                    if i == 8:
                        dve.wait_ge(lw_exp, 1)
                    for e in range(2):
                        h = 2 * a + e
                        v = lw[:, h, off:off + nk]
                        ins = dve.tensor_tensor_reduce(out=v, in0=ps[:, bank + e, 0:nk], in1=v, scale=BD ** -0.5,
                                                       scalar=0.0, op0=ALU.mult, op1=ALU.add,
                                                       accum_out=small[:, 64 + 4 * r + h:65 + 4 * r + h])
                    ins.then_inc(sc_read, 1)
                    return
                if kind == "X":
                    link(dve.tensor_reduce(nmax[:, col], s, AX_X, ALU.max, negate=True))
                    dve.tensor_scalar(nmax[:, col], nmax[:, col], SCALE, None, ALU.mult).then_inc(sc_read, 1)
                    return
                if kind == "R":
                    mask = toep[:, 2 * a:2 * a + 2, ::-1][:, :, SEQ - nk:SEQ]
                else:
                    c = (C_MA if kind == "A" else C_MB) + SEQ - nk
                    mask = cst[:, c:c + nk].unsqueeze(1).to_broadcast([P, 2, nk])
                dst = sc[:, i % 2, :].rearrange("p (e k) -> p e k", e=2)[:, :, 0:nk]
                if i >= 2:
                    dve.wait_ge(p_ready, SOFT[i - 2])
                link(dve.scalar_tensor_tensor(out=dst, in0=s, scalar=SCALE, in1=mask, op0=ALU.mult, op1=ALU.add))
                dve.tensor_reduce(nmax[:, col], dst, AX_X, ALU.max, negate=True).then_inc(sc_read, 1)

            def combine(i):
                kind, r, a, L = ITEMS[i]
                if kind != "D":
                    return
                nk = P * (r + 1)
                dve.wait_ge(p_ready, SOFT[i])
                link(dve.reciprocal(cf[:, 0:2], sums[:, 2 * i:2 * i + 2]))
                link(dve.tensor_scalar(cf[:, 2:3], cf[:, 1:2], lam[:, 4:5], None, ALU.mult))
                dve.wait_ge(pT_ready, i - 1)
                c = comb[:, i % 2, 0:nk]
                link(dve.tensor_scalar(c, pr[:, i % 2, 0:nk], cf[:, 0:1], None, ALU.mult))
                dve.scalar_tensor_tensor(out=c, in0=pr[:, i % 2, 256:256 + nk], scalar=cf[:, 2:3], in1=c,
                                         op0=ALU.mult, op1=ALU.add).then_inc(comb_ready, 1)

            def ffn(f, u0, follow):
                j0 = STEPS * f

                def hidden(J, u, bank):
                    dve.wait_ge(silu_done, J + 1)
                    dve.wait_ge(unit_used, u)
                    if not isinstance(J, int) or J > 0:
                        dve.wait_ge(h_ready, J)
                    dve.tensor_tensor(hid, sil, ps[:, bank + 1, :], ALU.mult).then_inc(h_mul, 1)

                def split(J, par):
                    dve.wait_ge(h_mul, J + 1)
                    dve.tensor_copy(hhi[:, par, :], hid).then_inc(h_hi, 1)
                    dve.wait_ge(h_hi, J + 1)
                    dve.tensor_tensor(hlo[:, par, :], hid, hhi[:, par, :], ALU.subtract).then_inc(h_ready, 1)

                hidden(j0, u0 + 2, 0)
                lo(u0 + 3)
                split(j0, 0)
                lo(u0 + 4)
                lo(u0 + 5)
                hidden(j0 + 1, u0 + 4, 2)
                lo(u0 + 6)
                split(j0 + 1, 1)
                lo(u0 + 7)
                with dve.Fori(0, (STEPS - 3) // 2) as i:
                    for k in range(2):
                        u = u0 + 5 + 3 * k
                        lo_at(i, u + 3)
                        hidden(i * 2 + (j0 + 2 + k), i * 6 + (u + 2), 2 * k)
                        lo_at(i, u + 4)
                        split(i * 2 + (j0 + 2 + k), k)
                        lo_at(i, u + 5)
                lo(u0 + 32)
                hidden(j0 + 10, u0 + 31, 0)
                split(j0 + 10, 0)
                for c in range(u0 + 33, u0 + 32 + follow):
                    lo(c)

            dve.wait_ge(cst_full, 16)
            for r in range(RT):
                scaled(N_MIX, res, xn, r)
            dve.wait_ge(wif_hi, 1)
            dve.tensor_tensor(wifl[:, :, :], wif[:, :, :], wifh[:, :, :], ALU.subtract).then_inc(wif_lo, 1)
            lo(0)
            turned(T_MIX)
            lo(1)
            lo(2)

            dve.wait_ge(bias_full, 48)
            dve.wait_ge(gate_ps, 1)
            iff = small[:, 24:40].rearrange("p (r g h) -> p r g h", r=RT, g=2)
            dve.tensor_tensor(small[:, 24:40].rearrange("p (r g) -> p r g", r=RT),
                              ps[:, 4, 0:16].rearrange("p (r g) -> p r g", r=RT),
                              bif[:, :].unsqueeze(1).to_broadcast([P, RT, 2 * BH]), ALU.add).then_inc(gate_dve, 1)
            dve.wait_ge(gate_dve, 1)
            i_pre, f_pre = iff[:, :, 0, :], iff[:, :, 1, :]

            def rh(c):
                return small[:, c:c + 8].rearrange("p (r h) -> p r h", r=RT)

            dve.scalar_tensor_tensor(out=rh(0), in0=f_pre, scalar=-1.0, in1=f_pre, op0=ALU.mult, op1=ALU.max)\
                .then_inc(gate_dve, 1)
            link(dve.tensor_scalar(rh(72), f_pre, 0.0, None, ALU.min))

            def conv(j):
                x = cin[:, j, :]
                o = qkb[:, j, :]
                link(dve.tensor_scalar(o, x, cw[:, 24 + j:25 + j], None, ALU.mult))
                for d in range(1, CONV):
                    c = 8 * (CONV - 1 - d) + j
                    ins = dve.scalar_tensor_tensor(out=o[:, d:SEQ], in0=x[:, 0:SEQ - d], scalar=cw[:, c:c + 1],
                                                   in1=o[:, d:SEQ], op0=ALU.mult, op1=ALU.add)
                    if d < CONV - 1:
                        link(ins)
                ins.then_inc(conv_ready, 1)

            for u in range(PROJ):
                lo(u + 3)
                if u == 0:
                    dve.wait_ge(gate_act, 1)
                    dve.tensor_tensor(small[:, 80:88], small[:, 72:80], small[:, 16:24], ALU.subtract)\
                        .then_inc(gate_dve, 1)
                    dve.wait_ge(gate_ps, 2)
                    dve.tensor_copy(cw[:, :], ps[:, 5, 0:32])
                    dve.wait_ge(gate_ps, 3)
                    link(dve.tensor_copy(small[:, 88:96], ps[:, 4, 64:72]))
                    link(dve.tensor_tensor(rh(96), i_pre, rh(88), ALU.subtract))
                    for r in range(RT):
                        dve.tensor_tensor(diag[:, r, :, :], ident.unsqueeze(1).to_broadcast([P, BH, P]),
                                          small[:, 96 + 4 * r:100 + 4 * r].unsqueeze(2).to_broadcast([P, BH, P]),
                                          ALU.mult).then_inc(gate_dve, 1)
                if u == 1:
                    dve.wait_ge(gate_ps, 4)
                    tri = cst[:, C_MA + P:C_MA + 2 * P].unsqueeze(1).to_broadcast([P, 2, P])
                    for b in range(2):
                        a = ps[:, 6 + b, :].rearrange("p (h s) -> p h s", h=2)
                        w = lw[:, 2 * b:2 * b + 2, :]
                        dve.tensor_tensor(w[:, :, 0:P], a[:, :, 0:P], tri, ALU.add)
                        dve.tensor_copy(w[:, :, P:2 * P], a[:, :, 0:P])
                        ins = dve.tensor_tensor(w[:, :, 2 * P:3 * P], a[:, :, P:2 * P], tri, ALU.add)
                    link(ins)
                    dve.tensor_reduce(small[:, 104:108], lw[:, :, 0:P], AX_X, ALU.max)
                    link(dve.tensor_reduce(small[:, 108:112], lw[:, :, P:3 * P], AX_X, ALU.max))
                    link(dve.tensor_scalar(small[:, 112:120], small[:, 104:112], 0.0, None, ALU.max))
                    dve.tensor_scalar(small[:, 40:48], small[:, 112:120], -1.0, None, ALU.mult).then_inc(gate_dve, 1)
                    dve.tensor_tensor(small[:, 48:56], small[:, 88:96], small[:, 112:120], ALU.add)\
                        .then_inc(gate_dve, 1)
                if u in (1, 3):
                    s = (u - 1) // 2
                    dve.wait_ge(stream_evac, 2 * s + 2)
                    for r in range(RT):
                        rotate(z1[:, r, s, :], AH, cst[:, C_COS + AD * r:C_COS + AD * r + AD],
                               cst[:, C_SIN + AD * r:C_SIN + AD * r + AD], sq[:, 0, :], sq[:, 1, :])\
                            .then_inc(rope_ready, 1)
                        dve.wait_ge(rope_ready, 2 * s + r + 1)
                if u == 4:
                    dve.wait_ge(rel_full, 16)
                    dve.tensor_copy(rele[0:SH, 0:256], relr[0:SH, 1:N_REL]).then_inc(ext_ready, 1)
                    dve.tensor_copy(rele[0:SH, 256:512], relr[0:SH, 256:257].to_broadcast([SH, 256]))\
                        .then_inc(ext_ready, 1)
                    dve.wait_ge(const_full, 16 * N_CONST)
                    for n in range(2):
                        dve.tensor_tensor_reduce(out=lamv[:, 2 * n, :], in0=lamv[:, 2 * n, :], in1=lamv[:, 2 * n + 1, :],
                                                 scale=1.0, scalar=0.0, op0=ALU.mult, op1=ALU.add,
                                                 accum_out=lam[:, n:n + 1]).then_inc(lam_in, 1)
                    dve.tensor_scalar(gsub[:, :], gsub[:, :], 1.0 - LAM_INIT, None, ALU.mult)
                    link(dve.tensor_copy(posf[:, :], posi[:, :]))
                    ang = trig[:, 0, :]
                    dve.tensor_scalar(ang[:, 0:32], cst[:, C_INV:C_INV + 32], posf[:, 0:1], None, ALU.mult)
                    link(dve.tensor_scalar(ang[:, 32:64], cst[:, C_INV:C_INV + 32], posf[:, 1:2], None, ALU.mult))
                    dve.tensor_scalar(trig[:, 1, :], ang, 1 / TWO_PI, 0.0, ALU.mult, ALU.add)
                    link(dve.tensor_scalar(trig[:, 2, :], ang, 1 / TWO_PI, 0.25, ALU.mult, ALU.add))
                    link(dve.tensor_scalar(trig[:, 1:3, :], trig[:, 1:3, :], ROUND, -ROUND, ALU.add, ALU.add))
                    for n in range(2):
                        src = ang
                        for part in (PI_1, PI_2, PI_3):
                            link(dve.scalar_tensor_tensor(out=trig[:, 3 + n, :], in0=trig[:, 1 + n, :], scalar=-part,
                                                          in1=src, op0=ALU.mult, op1=ALU.add))
                            src = trig[:, 3 + n, :]
                    link(dve.tensor_scalar(trig[:, 4, :], trig[:, 4, :], math.pi / 2, None, ALU.add))
                    for n in range(2):
                        dve.tensor_scalar(trig[:, 3 + n, :], trig[:, 3 + n, :], PI_LIM, -PI_LIM, ALU.min, ALU.max)\
                            .then_inc(trig_in, 1)
                if u == 6:
                    dve.wait_ge(lam_out, 1)
                    link(dve.tensor_tensor(lam[:, 5:6], lam[:, 3:4], lam[:, 2:3], ALU.subtract))
                    dve.tensor_scalar(lam[:, 4:5], lam[:, 5:6], -LAM_INIT, None, ALU.add)
                    dve.wait_ge(trig_out, 1)
                    sin = trig[:, 5, :].rearrange("p (r d) -> p r d", r=RT)
                    cos = trig[:, 6, :].rearrange("p (r d) -> p r d", r=RT)
                    for n, table in enumerate((ropeq, ropek)):
                        g = [headg[:, n, 32 * a:32 * a + 32].unsqueeze(1).to_broadcast([P, RT, 32]) for a in range(2)]
                        for a in range(2):
                            dve.tensor_tensor(table[:, 0, :, 32 * a:32 * a + 32], cos, g[a], ALU.mult)
                            ins = dve.scalar_tensor_tensor(out=table[:, 1, :, 32 * a:32 * a + 32], in0=sin,
                                                           scalar=1.0 if a else -1.0, in1=g[1 - a],
                                                           op0=ALU.mult, op1=ALU.mult)
                    link(ins)
                if u >= 7:
                    k = u - 7
                    if k < 12:
                        scores(k)
                    if 2 <= k < 6:
                        dve.wait_ge(stream_evac, 6 + k - 1)
                        conv(2 * (k - 2))
                        conv(2 * (k - 2) + 1)
                    if k in (5, 9):
                        r = (k - 5) // 4
                        i = 4 * r
                        link(dve.reciprocal(rec[:, 0:8], sums[:, 2 * i:2 * i + 8]))
                        dve.wait_ge(pv_ready, i + 4)
                        dve.tensor_tensor(xn[:, r, 0:512].rearrange("p (h d) -> p h d", d=AD),
                                          ps[:, 7, :].rearrange("p (h d) -> p h d", d=AD),
                                          rec[:, 0:8].unsqueeze(2).to_broadcast([P, AH, AD]), ALU.mult)\
                            .then_inc(o_evac, 1)
                    if k in (11, 13):
                        r = (k - 11) // 2
                        den = small[:, 64 + 4 * r:68 + 4 * r]
                        link(dve.scalar_tensor_tensor(out=rec[:, 8:12], in0=den, scalar=-1.0, in1=den,
                                                      op0=ALU.mult, op1=ALU.max))
                        link(dve.tensor_tensor(rec[:, 8:12], rec[:, 8:12], small[:, 56 + 4 * r:60 + 4 * r], ALU.max))
                        link(dve.reciprocal(rec[:, 12:16], rec[:, 8:12]))
                        y = xn[:, r, 512:1024]
                        y3 = y.rearrange("p (h d) -> p h d", d=BD)
                        dve.wait_ge(pv_ready, 10 + 2 * r)
                        dve.tensor_tensor(y3, ps[:, 7, :].rearrange("p (h d) -> p h d", d=BD),
                                          rec[:, 12:16].unsqueeze(2).to_broadcast([P, BH, BD]), ALU.mult)\
                            .then_inc(mh_ready, 1)
                        dve.wait_ge(mh_ready, r + 1)
                        head_sum(r, BH, BD)
                        dve.wait_ge(ob_ready, 1)
                        link(dve.tensor_tensor(y3, y3, head_rstd(r, BH, BD), ALU.mult))
                        link(dve.tensor_tensor(y, y, gml[:, :], ALU.mult))
                        dve.tensor_tensor(y, y, z1[:, r, 4, :], ALU.mult).then_inc(y_ready, 1)
            turned(T_Y0)

            def merge(b):
                v = slice(2 * b, 2 * b + 2)
                flat = lambda s: s[:, v, :].rearrange("p a b -> p (a b)")
                if b >= 2:
                    dve.wait_ge(merged_lo, b - 1)
                dve.tensor_tensor(sc[:, b % 2, :], ps[:, 4 + b, :], flat(sga), ALU.mult)
                link(dve.tensor_tensor(pr[:, b % 2, :], ps[:, b, :], flat(sgb), ALU.mult))
                dve.tensor_tensor(sc[:, b % 2, :], sc[:, b % 2, :], pr[:, b % 2, :], ALU.add)\
                    .then_inc(merged_sum, 1)

            def merged_rest(b):
                v = slice(2 * b, 2 * b + 2)
                flat = lambda s: s[:, v, :].rearrange("p a b -> p (a b)")
                dve.wait_ge(merged_hi, b + 1)
                h, l = (hhi[:, b, :], hlo[:, b, :]) if b < 2 else (flat(xhi), flat(xlo))
                dve.tensor_tensor(l, sc[:, b % 2, :], h, ALU.subtract).then_inc(merged_lo, 1)

            for m in range(2):
                lo(PROJ + 3 + 2 * m)
                lo(PROJ + 4 + 2 * m)
                dve.wait_ge(unit_used, PROJ + 2 * m + 2)
                merge(2 * m)
                merge(2 * m + 1)
                merged_rest(2 * m)
                merged_rest(2 * m + 1)

            def out_stream(w):
                for m in range(4):
                    lo(w + 3 + m)

            out_stream(WO[0])
            residual(R_WO0, WO[0] + 3, 1.0, (4, 0))
            for r in range(RT):
                scaled(N_FFN, res, xn, r)
            turned(T_FFN)

            for r in range(RT):
                scaled(N_MEM0, memx, memx, r)
            ffn(0, FFU[0], 3)
            turned(T_MEM0)
            residual(R_FF0, FFU[0] + 32, 1.0)
            for r in range(RT):
                scaled(N_FIN, res, res, r)
            for r in range(RT):
                scaled(N_F1, res, xn, r)

            def head_scale(e, v, n, copied):
                dve.wait_ge(stream_evac, copied)
                v3 = v.rearrange("p (h d) -> p h d", d=HD)
                return dve.tensor_tensor(v3, v3, head_rstd(e, n, HD), ALU.mult)

            for L in range(2):
                eb = 2 + 10 * L
                for m in range(3):
                    lo(MEMU[L] + 2 + m)
                for r in range(RT):
                    head_sum(eb + r, MH, HD)
                turned(T_F1 + 5 * L)
                for r in range(RT):
                    head_scale(eb + r, kv[:, r, 0:MW], MH, STREAM0[f"mem{L}"] + r + 1).then_inc(zn_ready, 1)
                ffn(1 + 2 * L, FFU[1 + 2 * L], 3)
                u = MIXU[L]
                residual(R_F1 + 3 * L, FFU[1 + 2 * L] + 32, 0.5)
                for r in range(RT):
                    scaled(N_M0 + 4 * L, res, xn, r)
                lo(u + 2)
                turned(T_M0 + 5 * L)
                for m in range(10):
                    lo(u + m + 3)
                    s = m // 2
                    if m % 2 and s != 3:
                        n = 8 if s < 3 else MH
                        e0 = eb + 2 + 2 * s if s < 3 else eb + 8
                        for r in range(RT):
                            head_sum(e0 + r, n, HD)
                        for r in range(RT):
                            v = z2[:, r, 512 * s:512 * s + 512] if s < 3 else z2[:, r, 3 * SW:ZW]
                            ins = head_scale(e0 + r, v, n, STREAM0[f"mix{L}"] + 2 * s + r + 1)
                            if L == 1 and s < 3:
                                link(ins)
                                parts = [[(0, 512, ropeq)], [(0, 256, ropeq), (256, 512, ropek)],
                                         [(0, 512, ropek)]][s]
                                for a, b, table in parts:
                                    ins = rotate(v[:, a:b], (b - a) // HD, table[:, 0, r, :], table[:, 1, r, :],
                                                 rt1[:, a:b], rt2[:, a:b])
                            ins.then_inc(zn_ready, 1)
                if L == 0:
                    dve.wait_ge(toep_ready, 1)
                i0 = IT0[L]
                for k in range(N_IT + 3):
                    if k < N_IT:
                        scores(i0 + k)
                    if 1 <= k <= N_IT:
                        combine(i0 + k - 1)
                    if k in (10, 18):
                        r = (k - 10) // 8
                        i = i0 + 8 * r
                        dve.wait_ge(p_ready, SOFT[i + 7])
                        link(dve.reciprocal(rec[:, 16:32], sums[:, 2 * i:2 * i + 16]))
                        dve.wait_ge(pv_ready, i + 8)
                        o = ps[:, 6:8, :].rearrange("p a b -> p (a b)")
                        if L == 0:
                            dve.tensor_tensor(xn[:, r, :].rearrange("p (h d) -> p h d", d=HD),
                                              o.rearrange("p (h d) -> p h d", d=HD),
                                              rec[:, 16:32].unsqueeze(2).to_broadcast([P, 16, HD]), ALU.mult)\
                                .then_inc(y_ready, 1)
                        else:
                            e = 22 + r
                            head_sum(e, DH, 2 * HD, SW)
                            dve.tensor_tensor(xn[:, r, SW:DM].rearrange("p (h d) -> p h d", d=HD),
                                              o[:, SW:DM].rearrange("p (h d) -> p h d", d=HD),
                                              rec[:, 28:32].unsqueeze(2).to_broadcast([P, MH, HD]), ALU.mult)
                            y3 = xn[:, r, 0:SW].rearrange("p (h d) -> p h d", d=2 * HD)
                            link(dve.tensor_tensor(y3, o[:, 0:SW].rearrange("p (h d) -> p h d", d=2 * HD),
                                                   head_rstd(e, DH, 2 * HD), ALU.mult))
                            dve.tensor_tensor(y3, y3, gsub[:, :].unsqueeze(1).to_broadcast([P, DH, 2 * HD]),
                                              ALU.mult).then_inc(y_ready, 1)
                turned(T_Y1 + 5 * L)
                out_stream(WO[1 + L])
                residual(R_WO1 + 3 * L, WO[1 + L] + 3, 1.0)
                for r in range(RT):
                    scaled(N_F2 + 4 * L, res, xn, r)
                turned(T_F2 + 5 * L)
                if L == 0:
                    for r in range(RT):
                        scaled(N_MEM1, memx, memx, r)
                    ffn(2, FFU[2], 3)
                    turned(T_MEM1)
                    residual(R_F2, FFU[2] + 32, 0.5)
                    for r in range(RT):
                        scaled(N_F3, res, xn, r)
                else:
                    ffn(4, FFU[4], 1)
                    residual(R_F4, FFU[4] + 32, 0.5)

        @block.tensor
        def _(pe):
            def three(o, stat, mov, start, stop):
                pe.matmul(o, stat[0], mov[0], start=start, stop=False)
                pe.matmul(o, stat[0], mov[1], start=False, stop=False)
                return pe.matmul(o, stat[1], mov[0], start=False, stop=stop)

            def w(slot, a, n):
                return whi[:, slot, a:a + n], wlo[:, slot, a:a + n]

            def x(k, a=0, n=SEQ):
                return xhi[:, k, a:a + n], xlo[:, k, a:a + n]

            def turn(T, src, ready, third=None):
                for b in range(4):
                    if b == 2 and third:
                        pe.wait_ge(*third)
                    for r in range(RT):
                        if b == 0:
                            pe.wait_ge(*ready[r])
                        for c in (2 * b, 2 * b + 1):
                            a = 256 * (c % 2) + P * r
                            ins = pe.transpose(ps[:, b, a:a + P], src[:, r, P * c:P * c + P], ident)
                    ins.then_inc(tr_ps, 1)

            def narrow(u, slot, bank, T=None):
                pe.wait_ge(lo_done, u + 1)
                for n in range(2):
                    for k in range(KC):
                        if T is not None and n == 0 and k % 2 == 0:
                            pe.wait_ge(xlo_done, 4 * T + k // 2 + 1)
                        ins = three(ps[:, bank, 256 * n:256 * n + 256], w(slot, 256 * k + P * n, P), x(k),
                                    k == 0, k == KC - 1)
                ins.then_inc(unit_used, 1)

            def wide(u, half, banks, T=None, free=None):
                pe.wait_ge(lo_done, u + 1)
                for r in range(RT):
                    if free and half == 0 and free[r]:
                        pe.wait_ge(*free[r])
                    for k in range(4):
                        if T is not None and r == 0 and k % 2 == 0:
                            pe.wait_ge(xlo_done, 4 * T + (4 * half + k) // 2 + 1)
                        ins = three(ps[:, banks[r], :], x(4 * half + k, P * r, P), w(u % 3, 512 * k, 512),
                                    half == 0 and k == 0, half == 1 and k == 3)
                ins.then_inc(unit_used, 1)

            def down(u, slot, banks, first, last, left):
                pe.wait_ge(lo_done, u + 1)
                for r in range(RT):
                    for c in range(2):
                        for n in range(2):
                            ins = three(ps[:, banks[r] + n, :], left(c, r), w(slot, 1024 * c + 512 * n, 512),
                                        first and c == 0, last and c == 1)
                    if last and r == 0:
                        ins.then_inc(acc0_ready, 1)
                ins.then_inc(unit_used, 1)

            def hidden(par):
                return lambda c, r: (hhi[:, par, 256 * c + P * r:256 * c + P * r + P],
                                     hlo[:, par, 256 * c + P * r:256 * c + P * r + P])

            def ffn(f, u0, T, between=None):
                j0 = STEPS * f

                def gate_up(J, u, slot, par, T=None, wait=True):
                    if wait:
                        pe.wait_ge(silu_done, J - 1)
                    narrow(u, slot, 2 * par, T)
                    if wait:
                        pe.wait_ge(h_mul, J - 1)
                    narrow(u + 1, (slot + 1) % 3, 2 * par + 1)

                def down_step(J, u, slot, par, first=False, last=False):
                    pe.wait_ge(h_ready, J + 1)
                    down(u, slot, (4, 6), first, last, hidden(par))

                gate_up(j0, u0, u0 % 3, 0, T, False)
                gate_up(j0 + 1, u0 + 2, (u0 + 2) % 3, 1, None, False)
                down_step(j0, u0 + 4, (u0 + 4) % 3, 0, first=True)
                with pe.Fori(0, (STEPS - 3) // 2) as i:
                    for k in range(2):
                        u = u0 + 5 + 3 * k
                        gate_up(i * 2 + (j0 + 2 + k), i * 6 + u, u % 3, k)
                        down_step(i * 2 + (j0 + 1 + k), i * 6 + (u + 2), (u + 2) % 3, 1 - k)
                gate_up(j0 + 10, u0 + 29, (u0 + 29) % 3, 0)
                down_step(j0 + 9, u0 + 31, (u0 + 31) % 3, 1)
                if between:
                    between()
                down_step(j0 + 10, u0 + 32, (u0 + 32) % 3, 0, last=True)

            def s_banks(i):
                return (4, 5) if ITEMS[i][3] < 0 else (2 * (i % 2), 2 * (i % 2) + 1)

            def item_scores(i):
                kind, r, a, L = ITEMS[i]
                nk = SEQ if kind == "X" else P * (r + 1)
                if L < 0 and i > 0:
                    pe.wait_ge(sc_read, i)
                if L >= 0 and i - IT0[L] >= 2:
                    pe.wait_ge(sc_read, i - 1)
                    pe.wait_ge(p_ready, SOFT[i - 2])
                if i == 8:
                    pe.wait_ge(qkb_ready, 1)
                for e in range(2):
                    if kind == "M":
                        lhs, rhs = qkb[:, 2 * a + e, P * r:P * r + P], qkb[:, BH + 2 * a + e, 0:nk]
                    else:
                        q, k, ka = {"A": (qT, kT, a), "X": (qmT, kmT, a)}.get(kind, (qkT, qkT, 6 + a))
                        lhs = q[HD * e:HD * e + HD, a, P * r:P * r + P]
                        rhs = k[HD * e:HD * e + HD, ka, 0:nk]
                    ins = pe.matmul(ps[:, s_banks(i)[e], 0:nk], lhs, rhs, start=True, stop=True)
                ins.then_inc(sc_ready, 1)

            def item_turn(i):
                kind, r, a, L = ITEMS[i]
                nb = 2 if kind == "X" else r + 1
                if kind == "M":
                    pe.wait_ge(sc_read, i + 1)
                elif kind == "D":
                    pe.wait_ge(comb_ready, DIFF[i])
                else:
                    pe.wait_ge(p_ready, SOFT[i])
                if L < 0:
                    bank = 6
                    if i > 0:
                        pe.wait_ge(pT_evac, i)
                else:
                    bank = 4 + i % 2
                    if i - IT0[L] >= 2:
                        pe.wait_ge(pT_evac, i - 1)
                for e in range(1 if kind == "D" else 2):
                    for b in range(nb):
                        if kind == "M":
                            src = lw[:, 2 * a + e, P * (r + b):P * (r + b) + P]
                        elif kind == "D":
                            src = comb[:, i % 2, P * b:P * b + P]
                        else:
                            src = pr[:, i % 2, 256 * e + P * b:256 * e + P * b + P]
                        c = P * (e * nb + b)
                        ins = pe.transpose(ps[:, bank, c:c + P], src, ident)
                ins.then_inc(pT_ready, 1)

            def item_pv(i):
                kind, r, a, L = ITEMS[i]
                nb = 2 if kind == "X" else r + 1
                pe.wait_ge(pT_evac, i + 1)
                if i in (4, 8):
                    pe.wait_ge(o_evac, i // 4)
                if i == 10:
                    pe.wait_ge(mh_ready, 1)
                if L >= 0 and i == IT0[L] + 8:
                    pe.wait_ge(y_ready, 2 * L + 3)
                for e in range(1 if kind == "D" else 2):
                    h = a if kind == "D" else 2 * a + e
                    size = P if kind in "MD" else HD
                    o0 = size * h + (SW if kind == "X" else 0)
                    bank, col = (7, o0) if L < 0 else (6 + o0 // 512, o0 % 512)
                    for b in range(nb):
                        v = {"A": z1[:, b, 2, :], "M": z1[:, b, 3, :], "X": kv[:, b, MW:2 * MW],
                             "R": z2[:, b, 2 * SW:3 * SW], "D": z2[:, b, 2 * SW:3 * SW]}[kind]
                        c = P * (e * nb + b)
                        ins = pe.matmul(ps[:, bank, col:col + size], pT[:, i % 2, c:c + P],
                                        v[:, size * h:size * h + size], start=(b == 0), stop=(b == nb - 1))
                ins.then_inc(pv_ready, 1)

            pe.wait_ge(cst_full, 16)
            turn(T_MIX, xn, [(xn_ready, 2 * N_MIX + r + 1) for r in range(RT)])
            pe.wait_ge(wif_lo, 1)
            pe.wait_ge(xlo_done, 4 * T_MIX + 4)
            for r in range(RT):
                for k in range(KC):
                    ins = three(ps[:, 4, 8 * r:8 * r + 8], x(k, P * r, P), (wifh[:, k, :], wifl[:, k, :]),
                                k == 0, k == KC - 1)
            ins.then_inc(gate_ps, 1)
            tiles = 0
            for u in range(PROJ):
                free = lambda n: (stream_evac, n - 3) if n >= 4 else None
                if QKB <= u < VB or GA <= u:
                    if free(tiles):
                        pe.wait_ge(*free(tiles))
                    narrow(u, u % 3, tiles % 4)
                    tiles += 1
                else:
                    wide(u, u % 2, (tiles % 4, (tiles + 1) % 4), None, (free(tiles), free(tiles + 1)))
                    tiles += 2 * (u % 2)
                if u == 0:
                    pe.wait_ge(bias_full, 48)
                    pe.transpose(ps[:, 5, 0:32], cwr[:, :], ident[0:32, 0:32]).then_inc(gate_ps, 1)
                    pe.wait_ge(gate_dve, 3)
                    tri, ones = cst[:, C_TRI:C_TRI + P], cst[:, C_ONE:C_ONE + P]
                    pe.matmul(ps[:, 4, 64:68], tri, small[:, 80:84], start=True, stop=True)
                    pe.matmul(ps[:, 4, 68:72], ones, small[:, 80:84], start=True, stop=False)
                    pe.matmul(ps[:, 4, 68:72], tri, small[:, 84:88], start=False, stop=True).then_inc(gate_ps, 1)
                if u == 1:
                    pe.wait_ge(gate_dve, 5)
                    for h in range(BH):
                        for r in range(RT):
                            c = 256 * (h % 2) + P * r
                            ins = pe.matmul(ps[:, 6 + h // 2, c:c + P], ones, diag[:, r, h, :], start=True, stop=True)
                    ins.then_inc(gate_ps, 1)
                if u in (5, 6):
                    s = u - 5
                    pe.wait_ge(rope_ready, 2 * s + 2)
                    pe.wait_ge(gate_dve, 7)
                    for b in range(2):
                        for c in (2 * b, 2 * b + 1):
                            for r in range(RT):
                                a = 256 * (c % 2) + P * r
                                ins = pe.transpose(ps[:, 4 + 2 * s + b, a:a + P], z1[:, r, s, P * c:P * c + P], ident)
                        ins.then_inc(qk_ps, 1)
                if u == 7:
                    pe.wait_ge(qk_sb, 4)
                if u >= 7:
                    k = u - 7
                    if k < 12:
                        item_scores(k)
                    if 1 <= k <= 12:
                        item_turn(k - 1)
                    if 2 <= k <= 13:
                        item_pv(k - 2)
            pe.wait_ge(stream_evac, 22)
            turn(T_Y0, xn, [(y_ready, r + 1) for r in range(RT)])
            for m in range(4):
                u = PROJ + m
                pe.wait_ge(lo_done, u + 1)
                for n in range(4):
                    bank = 4 - 4 * (m % 2) + 2 * (m // 2) + n // 2
                    for k in range(4):
                        kk = k + 4 * (m % 2)
                        if n == 0 and k % 2 == 0:
                            pe.wait_ge(xlo_done, 4 * T_Y0 + kk // 2 + 1)
                        ins = three(ps[:, bank, 256 * (n % 2):256 * (n % 2) + 256], w(u % 3, 512 * k + P * n, P), x(kk),
                                    k == 0, k == 3)
                ins.then_inc(unit_used, 1)

            def merged(m):
                def left(c, r):
                    k = 2 * m + c
                    if m < 2:
                        a = 256 * c + P * r
                        return hhi[:, m, a:a + P], hlo[:, m, a:a + P]
                    return x(k, P * r, P)
                return left

            for m in range(4):
                pe.wait_ge(merged_lo, max(m + 1, 2))
                down(WO[0] + m, (WO[0] + m) % 3, (4, 0), m == 0, m == 3, merged(m))
            turn(T_FFN, xn, [(xn_ready, 2 * N_FFN + r + 1) for r in range(RT)])

            def turn_memory(L):
                pe.wait_ge(h_ready, STEPS * (1 + 2 * L))
                n = N_MEM0 + 5 * L
                turn(T_MEM0 + 5 * L, memx, [(xn_ready, 2 * n + r + 1) for r in range(RT)])

            def out_product(L):
                for m in range(4):
                    pe.wait_ge(xlo_done, 4 * (T_Y1 + 5 * L) + m + 1)
                    down(WO[1 + L] + m, (WO[1 + L] + m) % 3, (4, 6), m == 0, m == 3,
                         lambda c, r, m=m: x(2 * m + c, P * r, P))

            ffn(0, FFU[0], T_FFN, lambda: turn_memory(0))
            for L in range(2):
                T = T_MEM0 + 5 * L
                base = STREAM0[f"mem{L}"]
                pe.wait_ge(xlo_done, 4 * T + 4)
                for half in range(2):
                    wide(MEMU[L] + half, half, (2, 3))
                T = T_F1 + 5 * L
                n = N_F1 if L == 0 else N_F3
                turn(T, xn, [(xn_ready, 2 * n + r + 1) for r in range(RT)], third=(stream_evac, base + 2))
                ffn(1 + 2 * L, FFU[1 + 2 * L], T)
                T = T_M0 + 5 * L
                n = N_M0 if L == 0 else N_M1
                turn(T, xn, [(xn_ready, 2 * n + r + 1) for r in range(RT)])
                base, tb, zb = STREAM0[f"mix{L}"], 8 * L, 10 * L

                def turn_heads(tt, src, c0, ready):
                    pe.wait_ge(zn_ready, ready)
                    if tt >= 4:
                        pe.wait_ge(heads_sb, tb + tt - 3)
                    for c in range(2):
                        for r in range(RT):
                            a = 256 * c + P * r
                            ins = pe.transpose(ps[:, 4 + tt % 4, a:a + P], src[:, r, c0 + P * c:c0 + P * c + P], ident)
                    ins.then_inc(tr_heads, 1)

                for s in range(5):
                    free = [(stream_evac, base + 2 * s + r - 3) if 2 * s + r >= 4 else None for r in range(RT)]
                    for half in range(2):
                        wide(MIXU[L] + 2 * s + half, half, ((2 * s) % 4, (2 * s + 1) % 4), T if s == 0 else None, free)
                    if s == 0:
                        turn_heads(0, kv, 0, zb + 2)
                    if 1 <= s <= 3:
                        for b in range(2):
                            turn_heads(1 + 2 * (s - 1) + b, z2, 512 * (s - 1) + 256 * b, zb + 2 + 2 * s)
                turn_heads(7, z2, 3 * SW, zb + 10)
                pe.wait_ge(stream_evac, base + 10)
                pe.wait_ge(heads_sb, tb + 8)
                i0 = IT0[L]
                for k in range(N_IT + 3):
                    if k < N_IT:
                        item_scores(i0 + k)
                    if 2 <= k < N_IT + 2:
                        item_turn(i0 + k - 2)
                    if k >= 3:
                        item_pv(i0 + k - 3)
                turn(T_Y1 + 5 * L, xn, [(y_ready, 2 * L + 3 + r) for r in range(RT)])
                out_product(L)
                T = T_F2 + 5 * L
                n = N_F2 if L == 0 else N_F4
                turn(T, xn, [(xn_ready, 2 * n + r + 1) for r in range(RT)])
                ffn(2 + 2 * L, FFU[2 + 2 * L], T, (lambda: turn_memory(1)) if L == 0 else None)


_INS = ["x", "norm_mix_g", "w_in", "conv_w", "b_igate", "b_fgate", "mlstm_norm_g", "w_proj_a", "w_proj_b", "w_out",
        "norm_ffn_g", "w_gate_up", "w_down", "norm_final_g", "mem_2", "positions_2", "ffn1_norm_2", "ffn1_w_gate_2",
        "ffn1_w_up_2", "ffn1_w_down_2", "mix_norm_2", "mem_norm_2", "w_in_2", "w_mem_kv_2", "mem_q_norm_2",
        "mem_k_norm_2", "w_out_2", "a_q_norm_2", "a_k_norm_2", "a_rel_bias_2", "b_q_norm_2", "b_k_norm_2",
        "b_lambda_q1_2", "b_lambda_k1_2", "b_lambda_q2_2", "b_lambda_k2_2", "b_subln_2", "ffn2_norm_2",
        "ffn2_w_gate_2", "ffn2_w_up_2", "ffn2_w_down_2"]


def kernel(**inputs):
    import concourse.bacc as bacc
    from concourse.bass_utils import run_bass_kernel_spmd

    nc = bacc.Bacc("TRN2", target_bir_lowering=False, num_devices=1)
    arrays, aps = {}, {}
    given = {name: inputs[name] for name in _INS}
    given["consts"] = shape_constants()
    for name, a in given.items():
        a = np.ascontiguousarray(a)
        arrays[f"in_{name}"] = a
        aps[name] = nc.dram_tensor(f"in_{name}", a.shape, mybir.dt.from_np(a.dtype), kind="ExternalInput").ap()
    out = nc.dram_tensor("out", (1, SEQ, DM), F32, kind="ExternalOutput").ap()
    build(nc, aps, out)
    r = run_bass_kernel_spmd(nc, [arrays], core_ids=[0])
    return r.results[0]["out"]
```

```python
import math
from contextlib import ExitStack

import numpy as np

import concourse.bass as bass
from concourse import mybir

F32 = mybir.dt.float32
F32R = mybir.dt.float32r
I32 = mybir.dt.int32
ACT = mybir.ActivationFunctionType
ALU = mybir.AluOpType
AX_X = mybir.AxisListType.X

P = 128
SEQ = 256
DM = 1024
RT = SEQ // P
KC = DM // P
EPS = 1e-6
MASKED = -1e30

AH, AD = 8, 64
BH, BD = 4, 128
CONV = 4
FF = 2816
SH, MH, HD = 12, 4, 64
DH = SH // 2
SW, MW = SH * HD, MH * HD
ZW = 3 * SW + MW
N_REL, REL_CLIP = 257, 128
LAM_INIT = 0.8 - 0.6 * math.exp(-0.3)
SCALE = HD ** -0.5

UW = 2048
STEPS = FF // 256
FF_UNITS = 3 * STEPS
QA, KA, VA, QKB, VB, OB, GA, GB = 0, 2, 4, 6, 10, 12, 14, 18
PROJ = 22
WO = [26, 108, 190]
FFU = [30, 63, 112, 145, 194]
MIXU = [96, 178]
MEMU = [106, 188]
N_UNITS = FFU[4] + FF_UNITS
assert WO[0] + 4 == FFU[0] and FFU[0] + FF_UNITS == FFU[1] and FFU[1] + FF_UNITS == MIXU[0]
assert MIXU[0] + 10 == MEMU[0] and MEMU[0] + 2 == WO[1] and WO[1] + 4 == FFU[2]
assert FFU[2] + FF_UNITS == FFU[3] and FFU[3] + FF_UNITS == MIXU[1] and WO[2] + 4 == FFU[4]

N_MIX, N_FFN, N_FIN, N_F1, N_M0, N_MEM0, N_F2, N_F3, N_M1, N_MEM1, N_F4 = range(11)
T_MIX, T_Y0, T_FFN, T_F1, T_M0, T_MEM0, T_Y1, T_F2, T_F3, T_M1, T_MEM1, T_Y2, T_F4 = range(13)
TURN_BANKS = {T_FFN: (2, 3, 6, 7)}
TURN_BANKS.update({T_M0: (0, 1, 4, 5), T_M1: (0, 1, 4, 5)})
TURN_BANKS.update({T_MEM0: (2, 3, 2, 3), T_MEM1: (2, 3, 2, 3), T_Y1: (0, 1, 2, 3), T_Y2: (0, 1, 2, 3)})
R_WO0, R_FF0, R_F1, R_WO1, R_F2, R_F3, R_WO2, R_F4 = range(8)



def place(n, r):
    if n in (N_FIN, N_F1):
        return 2 * N_FIN + 2 * r + n - N_FIN
    return 2 * n + r


ITEMS = [("A", rt, a, -1) for rt in range(RT) for a in range(AH // 2)]
ITEMS += [("M", rt, a, -1) for rt in range(RT) for a in range(BH // 2)]
for _layer, _kind in enumerate("RD"):
    ITEMS += [(_kind, rt, a, _layer) for rt in range(RT) for a in range(SH // 2)]
    ITEMS += [("X", rt, a, _layer) for rt in range(RT) for a in range(MH // 2)]
def s_bank(i):
    L = ITEMS[i][3]
    return 4 if L < 0 else 2 if i - IT0[L] in (13, 15) else 0


AHEAD = [(1, 11), (3, 12), (7, 13), (9, 14)]
MEM_AT = [4, 6, 7, 8]
IT0 = [12, 28]
N_IT = 16
SOFT = np.cumsum([k != "M" for k, *_ in ITEMS]).tolist()
DIFF = np.cumsum([k == "D" for k, *_ in ITEMS]).tolist()
STREAM0 = {"mix0": 22, "mem0": 32, "mix1": 34, "mem1": 44}

C_ID, C_MA, C_TRI, C_ONE, C_COS, C_SIN, C_MB, C_INV = 0, 128, 384, 512, 640, 768, 896, 1152
C_W = 1184


def shape_constants():
    c = np.zeros((P, C_W), np.float32)
    i = np.arange(P)
    c[:, C_ID:C_ID + P] = np.eye(P)
    c[:, C_MA + P:C_MA + 2 * P] = np.where(i[None, :] > i[:, None], MASKED, 0.0)
    c[:, C_TRI:C_TRI + P] = i[:, None] <= i[None, :]
    c[:, C_ONE:C_ONE + P] = 1.0
    half = AD // 2
    inv = np.float32(10000.0) ** (-np.arange(half, dtype=np.float32) / np.float32(half))
    for rt in range(RT):
        ang = ((rt * P + i).astype(np.float32)[:, None] * inv[None, :]).astype(np.float64)
        c[:, C_COS + rt * AD:C_COS + rt * AD + AD] = np.concatenate([np.cos(ang)] * 2, 1)
        c[:, C_SIN + rt * AD:C_SIN + rt * AD + AD] = np.concatenate([-np.sin(ang), np.sin(ang)], 1)
    c[0:64, C_MB + P + 64:C_MB + 2 * P] = MASKED
    c[:, C_INV:C_INV + 32] = np.float32(1.0) / (
        np.float32(10000.0) ** (np.arange(0, HD, 2, dtype=np.float32) / np.float32(HD)))
    return c


def build(nc, t, out):
    TWO_PI = 2 * math.pi
    PI_1 = 6.28125
    PI_2 = math.floor((TWO_PI - PI_1) * 2 ** 21) / 2 ** 21
    PI_3 = TWO_PI - PI_1 - PI_2
    ROUND = 12582912.0
    PI_LIM = 3.1415925

    with ExitStack() as ctx:
        def sb(name, shape, dt=F32):
            return ctx.enter_context(nc.sbuf_tensor(name, shape, dt))

        def sem(name):
            return ctx.enter_context(nc.semaphore(name))

        raw = sb("raw", [P, 3, UW])
        whi = sb("whi", [P, 3, UW], F32R)
        wlo = sb("wlo", [P, 3, UW], F32R)
        xhi = sb("xhi", [P, KC, SEQ], F32R)
        xlo = sb("xlo", [P, KC, SEQ], F32R)
        hhi = sb("hhi", [P, 2, 512], F32R)
        hlo = sb("hlo", [P, 2, 512], F32R)
        res = sb("res", [P, RT, DM])
        xn = sb("xn", [P, RT, DM])
        gain = sb("gain", [P, 2, DM])
        work = sb("work", [P, 10752])
        sc = sb("sc", [P, 2, 512])
        pr = sb("pr", [P, 2, 512])
        pT = sb("pT", [P, 2, 512])
        sq = sb("sq", [P, 2, 512])
        cst = sb("cst", [P, C_W])
        wif = sb("wif", [P, KC, 2 * BH])
        wifs = sb("wifs", [P, KC, 4 * BH], F32R)
        bif = sb("bif", [P, 2 * BH])
        cwr = sb("cwr", [32, P])
        cw = sb("cw", [P, 32])
        gml = sb("gml", [P, BH * BD])
        colg = sb("colg", [P, 8])
        headg = sb("headg", [P, 2, HD])
        lam = sb("lam", [P, 8])
        gsub = sb("gsub", [P, 2 * HD])
        posi = sb("posi", [P, RT], I32)
        posf = sb("posf", [P, RT])
        ropeq = sb("ropeq", [P, 2, RT, HD])
        ropek = sb("ropek", [P, 2, RT, HD])
        small = sb("small", [P, 160])
        ss = sb("ss", [P, 44])
        ms = sb("ms", [P, 22])
        rstd = sb("rstd", [P, 22])
        hss = sb("hss", [P, 4, 8])
        hms = sb("hms", [P, 4, 8])
        hrs = sb("hrs", [P, 4, 8])
        mhalf = sb("mhalf", [P, 1])
        sums = sb("sums", [P, 2 * len(ITEMS)])
        nmax = sb("nmax", [P, 2 * len(ITEMS)])
        rec = sb("rec", [P, 48])
        cf = sb("cf", [P, 4])

        with nc.sbuf_tensor("first", [P, 2048], F32) as first, nc.sbuf_tensor("turned_a", [P, 2, 4, SEQ], F32R) as turned_a:
            qT, kT = turned_a[:, 0, :, :], turned_a[:, 1, :, :]
        heads_t = sb("heads_t", [P, 16, SEQ], F32R)

        ps = ctx.enter_context(nc.psum_tensor("ps", [P, 8, 512], F32))
        relx = nc.dram_tensor("relx", [SH, 512], F32).ap()

        def region(off, *shape, of=None):
            n = int(np.prod(shape))
            v = (of or work)[:, off:off + n]
            if len(shape) == 2:
                v = v.rearrange("p (a b) -> p a b", b=shape[1])
            if len(shape) == 3:
                v = v.rearrange("p (a b c) -> p a b c", b=shape[1], c=shape[2])
            return v

        z1 = region(0, RT, 5, 512)
        qkb = region(5120, 2 * BH, SEQ)
        sga = region(7168, KC, SEQ)
        sgb = region(0, KC, SEQ, of=first)
        cin = region(0, 2 * BH, SEQ, of=first)
        diag = region(0, RT, BH, P, of=first)
        lw = region(9216, BH, 384)
        relr = region(7168, N_REL)
        rele = region(7168 + 260, 512)
        trig = region(7960, 7, 64)
        lamv = region(8408, 4, HD)
        z2 = region(0, RT, ZW)
        kv = region(5120, RT, 512)
        toep = region(6144, SH, SEQ)
        rt1 = region(6144, 512)
        rt2 = region(6656, 512)
        comb = region(9216, 2, SEQ)
        qkT = heads_t[:, 0:12, :]
        a_lo = (hhi[:, :, :], hlo[:, :, :])
        qk_lo = (heads_t[:, 12:16, :].rearrange("p (a b) c -> p a (b c)", a=2), hhi[:, :, :], hlo[:, :, :])
        qmT, kmT, qm_lo, km_lo = xhi[:, 0:2, :], xhi[:, 2:4, :], xlo[:, 0:2, :], xlo[:, 2:4, :]
        sil = pr[:, 0, :]
        hid = sc[:, 0, :]

        ident = cst[:, C_ID:C_ID + P]

        const_full, cst_full, wif_full = sem("const_full"), sem("cst_full"), sem("wif_full")
        ident_full = sem("ident_full")
        half_full, half_hi, half_lo = sem("half_full"), sem("half_hi"), sem("half_lo")
        x_full = [sem(f"x_full{r}") for r in range(RT)]
        raw_full = [sem(f"raw_full{s}") for s in range(3)]
        gain_full = [sem(f"gain_full{s}") for s in range(2)]
        mem_full, toep_full, rel_full, relx_full = sem("mem_full"), sem("toep_full"), sem("rel_full"), sem("relx_full")
        out_full = sem("out_full")
        hi_done, lo_done, unit_used = sem("hi_done"), sem("lo_done"), sem("unit_used")
        sq_done, rstd_ready, xn_ready, pool_ms = sem("sq_done"), sem("rstd_ready"), sem("xn_ready"), sem("pool_ms")
        tr_ps, xhi_done, xlo_done = sem("tr_ps"), sem("xhi_done"), sem("xlo_done")
        acc_ready, res_done = sem("acc_ready"), sem("res_done")
        silu_done, h_mul, h_hi, h_ready = sem("silu_done"), sem("h_mul"), sem("h_hi"), sem("h_ready")
        stream_evac = sem("stream_evac")
        wif_hi, wif_lo = sem("wif_hi"), sem("wif_lo")
        gate_ps, gate_act, gate_dve = sem("gate_ps"), sem("gate_act"), sem("gate_dve")
        lw_exp = sem("lw_exp")
        dve_chain, act_chain, pool_chain = sem("dve_chain"), sem("act_chain"), sem("pool_chain")
        rope_ready, qk_ps, qk_sb = sem("rope_ready"), sem("qk_ps"), sem("qk_sb")
        conv_ready, qkb_ready, ob_ready = sem("conv_ready"), sem("qkb_ready"), sem("ob_ready")
        sc_ready, sc_read, p_ready, comb_ready = sem("sc_ready"), sem("sc_read"), sem("p_ready"), sem("comb_ready")
        pT_ready, pT_evac, pv_ready, o_evac = sem("pT_ready"), sem("pT_evac"), sem("pv_ready"), sem("o_evac")
        mh_ready, hsq_ready, hss_ready, hms_done, hrs_ready = (
            sem("mh_ready"), sem("hsq_ready"), sem("hss_ready"), sem("hms_done"), sem("hrs_ready"))
        zn_ready, y_ready = sem("zn_ready"), sem("y_ready")
        merged_sum, merged_hi, merged_lo = sem("merged_sum"), sem("merged_hi"), sem("merged_lo")
        toep_ready, trig_in, trig_out, lam_in, lam_out = (
            sem("toep_ready"), sem("trig_in"), sem("trig_out"), sem("lam_in"), sem("lam_out"))
        ext_ready, bias_full = sem("ext_ready"), sem("bias_full")
        tr_heads, heads_hi, heads_lo, qk_lo_done = sem("tr_heads"), sem("heads_hi"), sem("heads_lo"), sem("qk_lo_done")
        o_copied = sem("o_copied")
        N_CONST = 21

        def across(v):
            return bass.AP(tensor=v.tensor, offset=v.offset, ap=[[0, P]] + [list(x) for x in v.ap])

        block = ctx.enter_context(nc.Block())

        @block.sync
        def _(sp):
            def fill(u, slot, src, a):
                if not isinstance(u, int) or u >= 3:
                    sp.wait_ge(lo_done, u - 2)
                sp.dma_start(raw[:, slot, :].rearrange("p (a b) -> p a b", a=a), src)\
                    .then_inc(raw_full[slot], 16)

            def cols(w, k0, nk, c0, n):
                return w.rearrange("(k p) n -> p k n", p=P)[:, k0:k0 + nk, bass.ds(c0, n)]

            def rows(w, k0):
                return w.rearrange("(j c p) n -> p j (c n)", p=P, c=2)[:, bass.ds(k0, 1), :]

            def down(w, j):
                return w.rearrange("(j c p) n -> p j c n", p=P, c=2)[:, bass.ds(j, 1), :, :]\
                    .rearrange("p j c n -> p (j c) n")

            def wide(u, w, c0):
                for k in range(2):
                    fill(u + k, (u + k) % 3, cols(w, 4 * k, 4, c0, 512), 4)

            def ffn(u0, gate, g0, up, p0, dn):
                def gate_up(u, slot, j):
                    fill(u, slot, cols(gate, 0, KC, g0 + 256 * j, 256), KC)
                    fill(u + 1, (slot + 1) % 3, cols(up, 0, KC, p0 + 256 * j, 256), KC)
                gate_up(u0, u0 % 3, 0)
                gate_up(u0 + 2, (u0 + 2) % 3, 1)
                fill(u0 + 4, (u0 + 4) % 3, down(dn, 0), 2)
                with sp.Fori(0, (STEPS - 3) // 2) as i:
                    for k in range(2):
                        u = u0 + 5 + 3 * k
                        gate_up(i * 6 + u, u % 3, i * 2 + (2 + k))
                        fill(i * 6 + (u + 2), (u + 2) % 3, down(dn, i * 2 + (1 + k)), 2)
                gate_up(u0 + 29, (u0 + 29) % 3, STEPS - 1)
                for j in (STEPS - 2, STEPS - 1):
                    u = u0 + 31 + j - (STEPS - 2)
                    fill(u, u % 3, down(dn, j), 2)

            for r in range(RT):
                sp.dma_start(res[:, r, :], t["x"][0, r * P:(r + 1) * P, :]).then_inc(x_full[r], 16)
            w_in = t["w_in"][0]
            for h, s in enumerate((half_full, raw_full[0])):
                sp.dma_start(raw[:, 0, 1024 * h:1024 * h + 1024].rearrange("p (a b) -> p a b", a=2),
                             cols(w_in, 2 * h, 2, 0, 512)).then_inc(s, 16)
            fill(QA + 1, 1, cols(w_in, 4, 4, 0, 512), 4)
            wide(KA, w_in, 512)
            wide(VA, w_in, 1024)
            for n in range(4):
                fill(QKB + n, (QKB + n) % 3, cols(w_in, 0, KC, 1536 + 256 * n, 256), KC)
            wide(VB, w_in, 2560)
            wide(OB, w_in, 3072)
            for n in range(8):
                fill(GA + n, (GA + n) % 3, cols(w_in, 0, KC, 3592 + 256 * n, 256), KC)
            for m in range(4):
                w = t["w_proj_b" if m % 2 else "w_proj_a"][0]
                fill(PROJ + m, (PROJ + m) % 3, cols(w, 0, 4, 512 * (m // 2), 512), 4)
            for m in range(4):
                fill(WO[0] + m, (WO[0] + m) % 3, down(t["w_out"][0], m), 2)
            gu = t["w_gate_up"][0]
            ffn(FFU[0], gu, 0, gu, FF, t["w_down"][0])
            for L in range(2):
                ffn(FFU[1 + 2 * L], t["ffn1_w_gate_2"][L], 0, t["ffn1_w_up_2"][L], 0, t["ffn1_w_down_2"][L])
                for s in range(5):
                    wide(MIXU[L] + 2 * s, t["w_in_2"][L], 512 * s)
                wide(MEMU[L], t["w_mem_kv_2"][L], 0)
                for m in range(4):
                    fill(WO[1 + L] + m, (WO[1 + L] + m) % 3, down(t["w_out_2"][L], m), 2)
                ffn(FFU[2 + 2 * L], t["ffn2_w_gate_2"][L], 0, t["ffn2_w_up_2"][L], 0, t["ffn2_w_down_2"][L])
            for r in range(RT):
                for h in range(2):
                    sp.wait_ge(res_done, 4 * R_F4 + 2 * r + h + 1)
                    sp.dma_start(out[0, r * P:(r + 1) * P, 512 * h:512 * h + 512], res[:, r, 512 * h:512 * h + 512])\
                        .then_inc(out_full, 16)
            sp.wait_ge(out_full, 16 * 2 * RT)

        @block.gpsimd
        def _(pool):
            def load(dst, src):
                pool.dma_start(dst, src).then_inc(const_full, 16)

            norm_gain = [t["norm_mix_g"][0], t["norm_ffn_g"][0], t["norm_final_g"]]
            for L in range(2):
                norm_gain += [t[v][L] for v in ("ffn1_norm_2", "mix_norm_2", "mem_norm_2", "ffn2_norm_2")]

            def load_gain(n):
                if n >= 2:
                    pool.wait_ge(xn_ready, 2 * place(n - 2, 1) + 2)
                pool.dma_start(gain[:, n % 2, :], across(norm_gain[n])).then_inc(gain_full[n % 2], 16)

            def norm(*ns):
                for c in [place(n, r) for r in range(RT) for n in ns]:
                    pool.wait_ge(sq_done, 2 * c + 2)
                    pool.tensor_scalar(ms[:, c:c + 1], ss[:, 2 * c:2 * c + 1], ss[:, 2 * c + 1:2 * c + 2], EPS,
                                       ALU.add, ALU.add)\
                        .then_inc(pool_ms, 1)
                    pool.wait_ge(pool_ms, c + 1)
                    pool.tensor_tensor(rstd[:, c:c + 1], ms[:, c:c + 1], mhalf[:, :], ALU.pow)\
                        .then_inc(rstd_ready, 1)

            def head_norm(e, n, size):
                pool.wait_ge(hss_ready, e + 1)
                pool.tensor_scalar(hms[:, e % 4, 0:n], hss[:, e % 4, 0:n], 1.0 / size, EPS, ALU.mult, ALU.add)\
                    .then_inc(hms_done, 1)
                pool.wait_ge(hms_done, e + 1)
                pool.tensor_tensor(hrs[:, e % 4, 0:n], hms[:, e % 4, 0:n], mhalf[:, :].to_broadcast([P, n]),
                                   ALU.pow).then_inc(hrs_ready, 1)

            pool.memset(mhalf[:, :], -0.5).then_inc(pool_chain, 1)
            load_gain(0)
            pool.wait_ge(pool_chain, 1)
            norm(N_MIX)
            load_gain(1)
            load(gml[:, :], across(t["mlstm_norm_g"][0]))
            with nc.allow_non_contiguous_dma(reason="small"):
                load(posi[:, :], t["positions_2"].rearrange("a (r p) -> p (a r)", p=P))
                col = [t["a_q_norm_2"][0], t["a_k_norm_2"][0], t["mem_q_norm_2"][0], t["mem_k_norm_2"][0],
                       t["mem_q_norm_2"][1], t["mem_k_norm_2"][1]]
                pool.dma_start(relr[0:SH, :], t["a_rel_bias_2"][0]).then_inc(rel_full, 16)
                for n, v in enumerate(col):
                    for half in range(2):
                        load(colg[HD * half:HD * half + HD, n:n + 1], v.rearrange("(p a) -> p a", a=1))
            for n, v in enumerate(["b_q_norm_2", "b_k_norm_2"]):
                load(headg[:, n, :], across(t[v][0]))
            for n, v in enumerate(["b_lambda_q1_2", "b_lambda_k1_2", "b_lambda_q2_2", "b_lambda_k2_2"]):
                load(lamv[:, n, :], across(t[v][0]))
            load(gsub[:, :], across(t["b_subln_2"][0]))

            pool.wait_ge(ext_ready, 2)
            pool.dma_start(relx, rele[0:SH, :]).then_inc(relx_full, 16)
            for e in range(2):
                head_norm(e, BH, BD)
            load_gain(2)
            norm(N_FFN)
            pool.wait_ge(merged_lo, 4)
            pool.wait_ge(relx_full, 16)
            diagonals = bass.AP(tensor=relx.tensor, offset=0, ap=[[1, P], [512, SH], [1, SEQ]])
            pool.dma_start(toep, diagonals).then_inc(toep_full, 16)
            pool.wait_ge(toep_full, 16)
            pool.memset(toep[0:64, :, 0:64], MASKED).then_inc(toep_ready, 1)
            for L in range(2):
                if L == 0:
                    load_gain(N_F1)
                    norm(N_FIN, N_F1)
                else:
                    norm(N_F3)
                load_gain(N_M0 + 4 * L)
                load_gain(N_MEM0 + 4 * L)
                norm(N_M0 + 4 * L)
                pool.wait_ge(tr_ps, 4 * (T_M0 + 5 * L) + 4)
                pool.dma_start(xn[:, :, :], t["mem_2"][0].rearrange("(r p) d -> p r d", p=P)).then_inc(mem_full, 16)
                load_gain(N_F2 + 4 * L)
                eb = 2 + 10 * L
                for e in range(6):
                    head_norm(eb + e, 8, HD)
                    if e == 1:
                        norm(N_MEM0 + 4 * L)
                if L == 0:
                    load_gain(N_F3)
                for e in range(6, 10):
                    head_norm(eb + e, MH, HD)
                if L == 1:
                    for e in range(2):
                        head_norm(22 + e, DH, 2 * HD)
                norm(N_F2 + 4 * L)

        @block.scalar
        def _(act):
            def hi(u, slot, half=None):
                if half != 1:
                    act.wait_ge(raw_full[slot], 16 * (u // 3 + 1))
                    if u >= 3:
                        act.wait_ge(unit_used, u - 2)
                v = slice(0, UW) if half is None else slice(1024 * half, 1024 * half + 1024)
                ins = act.activation(whi[:, slot, v], raw[:, slot, v], ACT.Copy)
                if half != 0:
                    ins.then_inc(hi_done, 1)

            def hi_at(i, c):
                act.wait_ge(raw_full[c % 3], i * 32 + 16 * (c // 3 + 1))
                act.wait_ge(unit_used, i * 6 + (c - 2))
                act.activation(whi[:, c % 3, :], raw[:, c % 3, :], ACT.Copy).then_inc(hi_done, 1)

            def square(n, src, r, ready=None, junk=None):
                for h in range(2):
                    if ready:
                        act.wait_ge(ready[0], ready[1] + h + 1)
                    c = 2 * place(n, r) + h
                    v = slice(512 * h, 512 * h + 512)
                    act.activation(xn[:, r, v] if junk is None else junk[:, h, :], src[:, r, v], ACT.Square, scale=DM ** -0.5,
                                   accum_out=ss[:, c:c + 1]).then_inc(sq_done, 1)

            def turned(T, parts=range(4)):
                for b in parts:
                    act.wait_ge(tr_ps, 4 * T + b + 1)
                    bank = TURN_BANKS.get(T, range(4))[b]
                    act.activation(xhi[:, 2 * b:2 * b + 2, :].rearrange("p a b -> p (a b)"), ps[:, bank, :], ACT.Copy)\
                        .then_inc(xhi_done, 1)

            def head_square(e, src, n):
                if e >= 2:
                    act.wait_ge(hss_ready, e - 1)
                act.activation(sq[:, e % 2, 0:n], src, ACT.Square).then_inc(hsq_ready, 1)

            def exps(i):
                kind, r, a, L = ITEMS[i]
                nk = SEQ if kind == "X" else P * (r + 1)
                act.wait_ge(sc_read, i + 1)
                if i >= 2:
                    act.wait_ge(pT_ready, i - 1)
                for e in range(2):
                    src = ps[:, s_bank(i) + e, 0:nk] if kind == "X" else sc[:, i % 2, 256 * e:256 * e + nk]
                    ins = act.activation(pr[:, i % 2, 256 * e:256 * e + nk], src, ACT.Exp,
                                         bias=nmax[:, 2 * i + e:2 * i + e + 1],
                                         scale=SCALE if kind == "X" else 1.0,
                                         accum_out=sums[:, 2 * i + e:2 * i + e + 1])
                ins.then_inc(p_ready, 1)

            def evac_pT(i):
                kind, r, a, L = ITEMS[i]
                n = (1 if kind == "D" else 2) * (2 if kind == "X" else r + 1) * P
                bank = 6 if L < 0 else 4 + i % 2
                act.wait_ge(pT_ready, i + 1)
                if i >= 2:
                    act.wait_ge(pv_ready, i - 1)
                act.activation(pT[:, i % 2, 0:n], ps[:, bank, 0:n], ACT.Copy).then_inc(pT_evac, 1)

            def ffn(f, u0, follow):
                j0 = STEPS * f

                def silu(J, u, bank):
                    act.wait_ge(unit_used, u)
                    if not isinstance(J, int) or J > 0:
                        act.wait_ge(h_mul, J)
                    act.activation(sil, ps[:, bank, :], ACT.Silu).then_inc(silu_done, 1)

                silu(j0, u0 + 1, 0)
                hi(u0 + 3, (u0 + 3) % 3)
                hi(u0 + 4, (u0 + 4) % 3)
                silu(j0 + 1, u0 + 3, 2)
                for c in range(u0 + 5, u0 + 8):
                    hi(c, c % 3)
                with act.Fori(0, (STEPS - 3) // 2) as i:
                    for k in range(2):
                        silu(i * 2 + (j0 + 2 + k), i * 6 + (u0 + 6 + 3 * k), 2 * k)
                        for c in range(u0 + 8 + 3 * k, u0 + 11 + 3 * k):
                            hi_at(i, c)
                silu(j0 + STEPS - 1, u0 + 30, 0)
                for c in range(u0 + 32, u0 + 32 + follow):
                    hi(c, c % 3)

            act.dma_start(cst[:, 0:P], t["consts"][:, 0:P]).then_inc(ident_full, 16)
            with nc.allow_non_contiguous_dma(reason="small"):
                act.dma_start(wif[:, :, :], t["w_in"][0].rearrange("(k p) n -> p k n", p=P)[:, :, 3584:3592])\
                    .then_inc(wif_full, 16)
            for r in range(RT):
                act.wait_ge(x_full[r], 16)
                square(N_MIX, res, r)
            act.dma_start(bif[:, 0:BH], across(t["b_igate"][0])).then_inc(bias_full, 16)
            act.dma_start(bif[:, BH:2 * BH], across(t["b_fgate"][0])).then_inc(bias_full, 16)
            act.dma_start(cwr[:, :], t["conv_w"][0].rearrange("j (c p) -> (j c) p", p=P)).then_inc(bias_full, 16)
            act.dma_start(cst[:, P:C_W], t["consts"][:, P:C_W]).then_inc(cst_full, 16)
            act.wait_ge(half_full, 16)
            act.activation(whi[:, 0, 0:1024], raw[:, 0, 0:1024], ACT.Copy).then_inc(half_hi, 1)
            turned(T_MIX)
            act.wait_ge(raw_full[0], 16)
            act.activation(whi[:, 0, 1024:2048], raw[:, 0, 1024:2048], ACT.Copy).then_inc(hi_done, 1)
            act.wait_ge(wif_full, 16)
            act.activation(wifs[:, :, 0:8], wif[:, :, :], ACT.Copy).then_inc(wif_hi, 1)
            hi(1, 1)
            hi(2, 2)

            def evac(n, dst, func=ACT.Copy):
                act.activation(dst, ps[:, n % 4, :], func).then_inc(stream_evac, 1)

            for u in range(PROJ):
                hi(u + 3, u % 3)
                if u == 1:
                    act.wait_ge(gate_dve, 2)
                    act.activation(small[:, 8:16], small[:, 0:8], ACT.Exp, scale=-1.0).then_inc(act_chain, 1)
                    act.wait_ge(act_chain, 1)
                    act.activation(small[:, 16:24], small[:, 8:16], ACT.Ln, bias=1.0).then_inc(gate_act, 1)
                act.wait_ge(unit_used, u + 1)
                if u in (QA + 1, KA + 1, VA + 1, VB + 1, OB + 1):
                    s = {QA: 0, KA: 1, VA: 2, VB: 3, OB: 4}[u - 1]
                    n0 = {0: 0, 1: 2, 2: 4, 3: 10, 4: 12}[s]
                    for r in range(RT):
                        evac(n0 + r, z1[:, r, s, :])
                if QKB <= u < VB:
                    j = u - QKB
                    evac(6 + j, cin[:, 2 * j:2 * j + 2, :].rearrange("p a b -> p (a b)"))
                if u == 4:
                    act.wait_ge(gate_dve, 7)
                    for r in range(RT):
                        for h in range(BH):
                            v = lw[:, h, 0:P] if r == 0 else lw[:, h, P:3 * P]
                            act.activation(v, v, ACT.Exp, bias=small[:, 40 + 4 * r + h:41 + 4 * r + h])
                    act.activation(small[:, 56:64], small[:, 48:56], ACT.Exp, scale=-1.0).then_inc(lw_exp, 1)
                if u in (5, 6):
                    for b in range(2):
                        n = 2 * (u - 5) + b
                        act.wait_ge(qk_ps, n + 1)
                        dst = (qT, kT)[u - 5][:, 2 * b:2 * b + 2, :].rearrange("p a b -> p (a b)")
                        act.activation(dst, ps[:, 4 + n, :], ACT.Copy).then_inc(qk_sb, 1)
                if u >= 7:
                    k = u - 7
                    if 1 <= k <= 12:
                        evac_pT(k - 1)
                    if k < 8:
                        exps(k)
                if u == 5:
                    act.wait_ge(lam_in, 2)
                    act.activation(lam[:, 2:4], lam[:, 0:2], ACT.Exp).then_inc(lam_out, 1)
                    act.wait_ge(trig_in, 2)
                    act.activation(trig[:, 5:7, :], trig[:, 3:5, :], ACT.Sin).then_inc(trig_out, 1)
                if u == 14:
                    act.wait_ge(conv_ready, 8)
                    act.activation(qkb, qkb, ACT.Silu).then_inc(qkb_ready, 1)
                    act.activation(z1[:, :, 4, :], z1[:, :, 4, :], ACT.Sigmoid).then_inc(ob_ready, 1)
                if GA <= u < PROJ:
                    j = u - GA
                    if j == 0:
                        act.wait_ge(relx_full, 16)
                    dst = (sga, sgb)[j // 4][:, 2 * (j % 4):2 * (j % 4) + 2, :].rearrange("p a b -> p (a b)")
                    evac(14 + j, dst, ACT.Sigmoid)
                if u in (18, 20):
                    r = (u - 18) // 2
                    act.wait_ge(mh_ready, r + 1)
                    head_square(r, xn[:, r, 512:1024], 512)
            turned(T_Y0)
            for m in range(2):
                hi(PROJ + 3 + 2 * m, (PROJ + 3 + 2 * m) % 3)
                hi(PROJ + 4 + 2 * m, (PROJ + 4 + 2 * m) % 3)
                for b in range(2 * m, 2 * m + 2):
                    act.wait_ge(merged_sum, b + 1)
                    dst = hhi[:, b, :] if b < 2 else xhi[:, 2 * b:2 * b + 2, :].rearrange("p a b -> p (a b)")
                    act.activation(dst, sc[:, b % 2, :], ACT.Copy).then_inc(merged_hi, 1)

            def two(u):
                for c in (u, u + 1):
                    hi(c, c % 3)

            two(WO[0] + 3)
            for r in range(RT):
                square(N_FFN, res, r, (res_done, 4 * R_WO0 + 2 * r))
            turned(T_FFN)
            two(FFU[0] + 1)

            act.wait_ge(const_full, 16 * N_CONST)
            ffn(0, FFU[0], 2)
            for r in range(RT):
                square(N_FIN, res, r, (res_done, 4 * R_FF0 + 2 * r))
                square(N_F1, res, r, (xn_ready, 2 * place(N_FIN, r)))
            for L in range(2):
                turned(T_F1 + 5 * L)
                two(FFU[1 + 2 * L] + 1)
                ffn(1 + 2 * L, FFU[1 + 2 * L], 2)
                u = MIXU[L]
                for r in range(RT):
                    square(N_M0 + 4 * L, res, r, (res_done, 4 * (R_F1 + 3 * L) + 2 * r))
                turned(T_M0 + 5 * L)
                two(u + 1)
                eb, tb, sb0, i0 = 2 + 10 * L, 8 * L, STREAM0[f"mix{L}"], IT0[L]

                def heads(tt, bank, dst, g):
                    act.wait_ge(tr_heads, tb + tt + 1)
                    act.activation(dst.rearrange("p a b -> p (a b)"), ps[:, bank, :], ACT.Copy,
                                   scale=1.0 if g is None else colg[:, g:g + 1]).then_inc(heads_hi, 1)

                def rows(s):
                    act.wait_ge(unit_used, u + 2 * s + 2)
                    for r in range(RT):
                        bank = (2 * s + 2 + r) % 4 if s < 5 else 2 + r
                        if s < 3:
                            head_square(eb + 2 * s + r, ps[:, bank, :], 512)
                        if s == 4:
                            head_square(eb + 6 + r, ps[:, bank, 256:512], MW)
                        if s == 5:
                            head_square(eb + 8 + r, ps[:, bank, 0:MW], MW)
                        dst = z2[:, r, 512 * s:512 * s + 512] if s < 5 else kv[:, r, :]
                        act.activation(dst, ps[:, bank, :], ACT.Copy).then_inc(stream_evac, 1)

                for m in range(8):
                    s = m // 2
                    if m < 7:
                        hi(u + m + 3, (u + m) % 3)
                    if m == 2:
                        act.wait_ge(mem_full, 16 * (L + 1))
                        for r in range(RT):
                            square(N_MEM0 + 4 * L, xn, r, junk=(pr, sc)[r])
                    if m % 2:
                        rows(s)
                        if 1 <= s <= 3:
                            for b in range(2):
                                tt = 2 * (s - 1) + b
                                heads(tt, 4 + tt % 4, qkT[:, 2 * tt:2 * tt + 2, :],
                                      (0 if tt < 3 else 1) if L == 0 else None)
                hi(u + 10, (u + 10) % 3)
                for k in range(N_IT + 3):
                    if 2 <= k < N_IT + 2:
                        evac_pT(i0 + k - 2)
                    if k == 2:
                        rows(4)
                    if k in (3, 4):
                        turned(T_MEM0 + 5 * L, range(2 * (k - 3), 2 * (k - 3) + 2))
                    if k == 9:
                        rows(5)
                    if k == 11:
                        heads(6, 3, qmT, 2 + 2 * L)
                        heads(7, 2, kmT, 3 + 2 * L)
                    for k0, c in AHEAD:
                        if k in (k0, k0 + 1):
                            hi(u + c, (u + c) % 3, k - k0)
                    if k < N_IT:
                        exps(i0 + k)
                    if L == 1 and k in (12, 14):
                        r = (k - 12) // 2
                        act.wait_ge(o_copied, 4 + r)
                        act.wait_ge(hss_ready, 22 + r)
                        act.activation(sq[:, :, :].rearrange("p a b -> p (a b)")[:, 0:SW], xn[:, r, 0:SW],
                                       ACT.Square).then_inc(hsq_ready, 1)
                turned(T_Y1 + 5 * L)
                two(WO[1 + L] + 3)
                for r in range(RT):
                    square(N_F2 + 4 * L, res, r, (res_done, 4 * (R_WO1 + 3 * L) + 2 * r))
                turned(T_F2 + 5 * L)
                two(FFU[2 + 2 * L] + 1)
                if L == 0:
                    ffn(2, FFU[2], 2)
                    for r in range(RT):
                        square(N_F3, res, r, (res_done, 4 * R_F2 + 2 * r))
                else:
                    ffn(4, FFU[4], 1)

        @block.vector
        def _(dve):
            count = [0]

            def link(ins):
                count[0] += 1
                ins.then_inc(dve_chain, 1)
                dve.wait_ge(dve_chain, count[0])

            def lo(u, half=None):
                if half != 1:
                    dve.wait_ge(hi_done, u + 1)
                v = slice(0, UW) if half is None else slice(1024 * half, 1024 * half + 1024)
                ins = dve.tensor_tensor(wlo[:, u % 3, v], raw[:, u % 3, v], whi[:, u % 3, v], ALU.subtract)
                if half != 0:
                    ins.then_inc(lo_done, 1)

            def lo_at(i, c):
                dve.wait_ge(hi_done, i * 6 + (c + 1))
                dve.tensor_tensor(wlo[:, c % 3, :], raw[:, c % 3, :], whi[:, c % 3, :], ALU.subtract)\
                    .then_inc(lo_done, 1)

            def scaled(n, src, dst, r):
                c = place(n, r)
                dve.wait_ge(rstd_ready, c + 1)
                if r == 0:
                    dve.wait_ge(gain_full[n % 2], 16 * (n // 2 + 1))
                for h in range(2):
                    v = slice(512 * h, 512 * h + 512)
                    dve.scalar_tensor_tensor(out=dst[:, r, v], in0=src[:, r, v], scalar=rstd[:, c:c + 1],
                                             in1=gain[:, n % 2, v], op0=ALU.mult, op1=ALU.mult)\
                        .then_inc(xn_ready, 1)

            def turned(T, parts=range(4)):
                for b in parts:
                    dve.wait_ge(xhi_done, 4 * T + b + 1)
                    v = slice(2 * b, 2 * b + 2)
                    bank = TURN_BANKS.get(T, range(4))[b]
                    dve.tensor_tensor(xlo[:, v, :].rearrange("p a b -> p (a b)"), ps[:, bank, :],
                                      xhi[:, v, :].rearrange("p a b -> p (a b)"), ALU.subtract)\
                        .then_inc(xlo_done, 1)

            def head_sum(e, n, size, width=None):
                dve.wait_ge(hsq_ready, e + 1)
                src = sq[:, e % 2, 0:n * size] if width is None else sq[:, :, :].rearrange("p a b -> p (a b)")[:, 0:width]
                dve.tensor_reduce(hss[:, e % 4, 0:n], src.rearrange("p (h d) -> p h d", d=size), AX_X, ALU.add)\
                    .then_inc(hss_ready, 1)

            def head_rstd(e, n, size):
                dve.wait_ge(hrs_ready, e + 1)
                return hrs[:, e % 4, 0:n].unsqueeze(2).to_broadcast([P, n, size])

            def residual(idx, u_last, factor, r, banks=(4, 6)):
                for h in range(2):
                    if (r, h) < (1, 1):
                        dve.wait_ge(acc_ready, 3 * idx + 2 * r + h + 1)
                    else:
                        dve.wait_ge(unit_used, u_last + 1)
                    v = slice(512 * h, 512 * h + 512)
                    dve.scalar_tensor_tensor(out=res[:, r, v], in0=ps[:, banks[r] + h, :], scalar=factor,
                                             in1=res[:, r, v], op0=ALU.mult, op1=ALU.add).then_inc(res_done, 1)

            def rotate(v, h, cos, sin, t1, t2):
                n = h * HD
                v3 = v.rearrange("p (h d) -> p h d", d=HD)
                swapped = v.rearrange("p (h two d) -> p h two d", two=2, d=HD // 2)[:, :, ::-1, :]
                s4 = sin.rearrange("p (two d) -> p two d", two=2).unsqueeze(1).to_broadcast([P, h, 2, HD // 2])
                dve.tensor_tensor(t1[:, 0:n].rearrange("p (h d) -> p h d", d=HD), v3,
                                  cos.unsqueeze(1).to_broadcast([P, h, HD]), ALU.mult)
                link(dve.tensor_tensor(t2[:, 0:n].rearrange("p (h two d) -> p h two d", two=2, d=HD // 2),
                                       swapped, s4, ALU.mult))
                return dve.tensor_tensor(v, t1[:, 0:n], t2[:, 0:n], ALU.add)

            def scores(i):
                kind, r, a, L = ITEMS[i]
                nk = SEQ if kind == "X" else P * (r + 1)
                bank = s_bank(i)
                s = ps[:, bank:bank + 2, 0:nk]
                col = slice(2 * i, 2 * i + 2)
                dve.wait_ge(sc_ready, i + 1)
                if kind == "M":
                    off = P if r else 0
                    if i == 8:
                        dve.wait_ge(lw_exp, 1)
                    for e in range(2):
                        h = 2 * a + e
                        v = lw[:, h, off:off + nk]
                        ins = dve.tensor_tensor_reduce(out=v, in0=ps[:, bank + e, 0:nk], in1=v, scale=BD ** -0.5,
                                                       scalar=0.0, op0=ALU.mult, op1=ALU.add,
                                                       accum_out=small[:, 64 + 4 * r + h:65 + 4 * r + h])
                    ins.then_inc(sc_read, 1)
                    return
                if kind == "X":
                    link(dve.tensor_reduce(nmax[:, col], s, AX_X, ALU.max, negate=True))
                    dve.tensor_scalar(nmax[:, col], nmax[:, col], SCALE, None, ALU.mult).then_inc(sc_read, 1)
                    return
                if kind == "R":
                    mask = toep[:, 2 * a:2 * a + 2, ::-1][:, :, SEQ - nk:SEQ]
                else:
                    c = (C_MA if kind == "A" else C_MB) + SEQ - nk
                    mask = cst[:, c:c + nk].unsqueeze(1).to_broadcast([P, 2, nk])
                dst = sc[:, i % 2, :].rearrange("p (e k) -> p e k", e=2)[:, :, 0:nk]
                if i >= 2:
                    dve.wait_ge(p_ready, SOFT[i - 2])
                link(dve.scalar_tensor_tensor(out=dst, in0=s, scalar=SCALE, in1=mask, op0=ALU.mult, op1=ALU.add))
                dve.tensor_reduce(nmax[:, col], dst, AX_X, ALU.max, negate=True).then_inc(sc_read, 1)

            def combine(i):
                kind, r, a, L = ITEMS[i]
                if kind != "D":
                    return
                nk = P * (r + 1)
                dve.wait_ge(p_ready, SOFT[i])
                link(dve.reciprocal(cf[:, 0:2], sums[:, 2 * i:2 * i + 2]))
                link(dve.tensor_scalar(cf[:, 2:3], cf[:, 1:2], lam[:, 4:5], None, ALU.mult))
                dve.wait_ge(pT_ready, i - 1)
                c = comb[:, i % 2, 0:nk]
                link(dve.tensor_scalar(c, pr[:, i % 2, 0:nk], cf[:, 0:1], None, ALU.mult))
                dve.scalar_tensor_tensor(out=c, in0=pr[:, i % 2, 256:256 + nk], scalar=cf[:, 2:3], in1=c,
                                         op0=ALU.mult, op1=ALU.add).then_inc(comb_ready, 1)

            def ffn(f, u0, follow):
                j0 = STEPS * f

                def hidden(J, u, bank):
                    dve.wait_ge(silu_done, J + 1)
                    dve.wait_ge(unit_used, u)
                    if not isinstance(J, int) or J > 0:
                        dve.wait_ge(h_ready, J)
                    dve.tensor_tensor(hid, sil, ps[:, bank + 1, :], ALU.mult).then_inc(h_mul, 1)

                def split(J, par):
                    dve.wait_ge(h_mul, J + 1)
                    dve.tensor_copy(hhi[:, par, :], hid).then_inc(h_hi, 1)
                    dve.wait_ge(h_hi, J + 1)
                    dve.tensor_tensor(hlo[:, par, :], hid, hhi[:, par, :], ALU.subtract).then_inc(h_ready, 1)

                hidden(j0, u0 + 2, 0)
                lo(u0 + 3)
                split(j0, 0)
                lo(u0 + 4)
                lo(u0 + 5)
                hidden(j0 + 1, u0 + 4, 2)
                lo(u0 + 6)
                split(j0 + 1, 1)
                lo(u0 + 7)
                with dve.Fori(0, (STEPS - 3) // 2) as i:
                    for k in range(2):
                        u = u0 + 5 + 3 * k
                        lo_at(i, u + 3)
                        hidden(i * 2 + (j0 + 2 + k), i * 6 + (u + 2), 2 * k)
                        lo_at(i, u + 4)
                        split(i * 2 + (j0 + 2 + k), k)
                        lo_at(i, u + 5)
                lo(u0 + 32)
                hidden(j0 + 10, u0 + 31, 0)
                split(j0 + 10, 0)
                for c in range(u0 + 33, u0 + 32 + follow):
                    lo(c)

            for r in range(RT):
                scaled(N_MIX, res, xn, r)
            dve.wait_ge(half_hi, 1)
            dve.tensor_tensor(wlo[:, 0, 0:1024], raw[:, 0, 0:1024], whi[:, 0, 0:1024], ALU.subtract).then_inc(half_lo, 1)
            turned(T_MIX)
            dve.wait_ge(hi_done, 1)
            dve.tensor_tensor(wlo[:, 0, 1024:2048], raw[:, 0, 1024:2048], whi[:, 0, 1024:2048], ALU.subtract)\
                .then_inc(lo_done, 1)
            dve.wait_ge(wif_hi, 1)
            dve.tensor_tensor(wifs[:, :, 8:16], wif[:, :, :], wifs[:, :, 0:8], ALU.subtract).then_inc(wif_lo, 1)
            lo(1)
            lo(2)
            dve.wait_ge(cst_full, 16)

            dve.wait_ge(bias_full, 48)
            dve.wait_ge(gate_ps, 1)
            iff = small[:, 24:40].rearrange("p (r g h) -> p r g h", r=RT, g=2)
            gates = small[:, 24:40].rearrange("p (r g) -> p r g", r=RT)
            parts = ps[:, 4, 0:32].rearrange("p (r two g) -> p r two g", r=RT, two=2)
            link(dve.tensor_tensor(gates, parts[:, :, 0, :], bif[:, :].unsqueeze(1).to_broadcast([P, RT, 2 * BH]),
                                   ALU.add))
            dve.tensor_tensor(gates, gates, parts[:, :, 1, :], ALU.add).then_inc(gate_dve, 1)
            dve.wait_ge(gate_dve, 1)
            i_pre, f_pre = iff[:, :, 0, :], iff[:, :, 1, :]

            def rh(c):
                return small[:, c:c + 8].rearrange("p (r h) -> p r h", r=RT)

            dve.scalar_tensor_tensor(out=rh(0), in0=f_pre, scalar=-1.0, in1=f_pre, op0=ALU.mult, op1=ALU.max)\
                .then_inc(gate_dve, 1)
            link(dve.tensor_scalar(rh(72), f_pre, 0.0, None, ALU.min))

            def conv(j):
                x = cin[:, j, :]
                o = qkb[:, j, :]
                link(dve.tensor_scalar(o, x, cw[:, 24 + j:25 + j], None, ALU.mult))
                for d in range(1, CONV):
                    c = 8 * (CONV - 1 - d) + j
                    ins = dve.scalar_tensor_tensor(out=o[:, d:SEQ], in0=x[:, 0:SEQ - d], scalar=cw[:, c:c + 1],
                                                   in1=o[:, d:SEQ], op0=ALU.mult, op1=ALU.add)
                    if d < CONV - 1:
                        link(ins)
                ins.then_inc(conv_ready, 1)

            for u in range(PROJ):
                lo(u + 3)
                if u == 1:
                    dve.wait_ge(gate_act, 1)
                    dve.tensor_tensor(small[:, 80:88], small[:, 72:80], small[:, 16:24], ALU.subtract)\
                        .then_inc(gate_dve, 1)
                    dve.wait_ge(gate_ps, 2)
                    dve.tensor_copy(cw[:, :], ps[:, 5, 0:32])
                if u == 2:
                    dve.wait_ge(gate_ps, 3)
                    link(dve.tensor_copy(small[:, 88:96], ps[:, 4, 64:72]))
                    link(dve.tensor_tensor(rh(96), i_pre, rh(88), ALU.subtract))
                    for r in range(RT):
                        dve.tensor_tensor(diag[:, r, :, :], ident.unsqueeze(1).to_broadcast([P, BH, P]),
                                          small[:, 96 + 4 * r:100 + 4 * r].unsqueeze(2).to_broadcast([P, BH, P]),
                                          ALU.mult).then_inc(gate_dve, 1)
                if u == 3:
                    dve.wait_ge(gate_ps, 4)
                    tri = cst[:, C_MA + P:C_MA + 2 * P].unsqueeze(1).to_broadcast([P, 2, P])
                    for b in range(2):
                        a = ps[:, 6 + b, :].rearrange("p (h s) -> p h s", h=2)
                        w = lw[:, 2 * b:2 * b + 2, :]
                        dve.tensor_tensor(w[:, :, 0:P], a[:, :, 0:P], tri, ALU.add)
                        dve.tensor_copy(w[:, :, P:2 * P], a[:, :, 0:P])
                        ins = dve.tensor_tensor(w[:, :, 2 * P:3 * P], a[:, :, P:2 * P], tri, ALU.add)
                    link(ins)
                    dve.tensor_reduce(small[:, 104:108], lw[:, :, 0:P], AX_X, ALU.max)
                    link(dve.tensor_reduce(small[:, 108:112], lw[:, :, P:3 * P], AX_X, ALU.max))
                    link(dve.tensor_scalar(small[:, 112:120], small[:, 104:112], 0.0, None, ALU.max))
                    dve.tensor_scalar(small[:, 40:48], small[:, 112:120], -1.0, None, ALU.mult).then_inc(gate_dve, 1)
                    dve.tensor_tensor(small[:, 48:56], small[:, 88:96], small[:, 112:120], ALU.add)\
                        .then_inc(gate_dve, 1)
                if u in (1, 3):
                    s = (u - 1) // 2
                    dve.wait_ge(stream_evac, 2 * s + 2)
                    for r in range(RT):
                        rotate(z1[:, r, s, :], AH, cst[:, C_COS + AD * r:C_COS + AD * r + AD],
                               cst[:, C_SIN + AD * r:C_SIN + AD * r + AD], sq[:, 0, :], sq[:, 1, :])\
                            .then_inc(rope_ready, 1)
                        dve.wait_ge(rope_ready, 2 * s + r + 1)
                if u == 4:
                    dve.wait_ge(rel_full, 16)
                    dve.tensor_copy(rele[0:SH, 0:256], relr[0:SH, 1:N_REL]).then_inc(ext_ready, 1)
                    dve.tensor_copy(rele[0:SH, 256:512], relr[0:SH, 256:257].to_broadcast([SH, 256]))\
                        .then_inc(ext_ready, 1)
                    dve.wait_ge(const_full, 16 * N_CONST)
                    for n in range(2):
                        dve.tensor_tensor_reduce(out=lamv[:, 2 * n, :], in0=lamv[:, 2 * n, :], in1=lamv[:, 2 * n + 1, :],
                                                 scale=1.0, scalar=0.0, op0=ALU.mult, op1=ALU.add,
                                                 accum_out=lam[:, n:n + 1]).then_inc(lam_in, 1)
                    dve.tensor_scalar(gsub[:, :], gsub[:, :], 1.0 - LAM_INIT, None, ALU.mult)
                    link(dve.tensor_copy(posf[:, :], posi[:, :]))
                    ang = trig[:, 0, :]
                    dve.tensor_scalar(ang[:, 0:32], cst[:, C_INV:C_INV + 32], posf[:, 0:1], None, ALU.mult)
                    link(dve.tensor_scalar(ang[:, 32:64], cst[:, C_INV:C_INV + 32], posf[:, 1:2], None, ALU.mult))
                    dve.tensor_scalar(trig[:, 1, :], ang, 1 / TWO_PI, 0.0, ALU.mult, ALU.add)
                    link(dve.tensor_scalar(trig[:, 2, :], ang, 1 / TWO_PI, 0.25, ALU.mult, ALU.add))
                    link(dve.tensor_scalar(trig[:, 1:3, :], trig[:, 1:3, :], ROUND, -ROUND, ALU.add, ALU.add))
                    for n in range(2):
                        src = ang
                        for part in (PI_1, PI_2, PI_3):
                            link(dve.scalar_tensor_tensor(out=trig[:, 3 + n, :], in0=trig[:, 1 + n, :], scalar=-part,
                                                          in1=src, op0=ALU.mult, op1=ALU.add))
                            src = trig[:, 3 + n, :]
                    link(dve.tensor_scalar(trig[:, 4, :], trig[:, 4, :], math.pi / 2, None, ALU.add))
                    for n in range(2):
                        dve.tensor_scalar(trig[:, 3 + n, :], trig[:, 3 + n, :], PI_LIM, -PI_LIM, ALU.min, ALU.max)\
                            .then_inc(trig_in, 1)
                if u in (5, 6):
                    for b in range(2):
                        n = 2 * (u - 5) + b
                        dve.wait_ge(qk_sb, n + 1)
                        src = (qT, kT)[u - 5][:, 2 * b:2 * b + 2, :].rearrange("p a b -> p (a b)")
                        dve.tensor_tensor(a_lo[u - 5][:, b, :], ps[:, 4 + n, :], src, ALU.subtract)\
                            .then_inc(qk_lo_done, 1)
                if u == 6:
                    dve.wait_ge(lam_out, 1)
                    link(dve.tensor_tensor(lam[:, 5:6], lam[:, 3:4], lam[:, 2:3], ALU.subtract))
                    dve.tensor_scalar(lam[:, 4:5], lam[:, 5:6], -LAM_INIT, None, ALU.add)
                    dve.wait_ge(trig_out, 1)
                    sin = trig[:, 5, :].rearrange("p (r d) -> p r d", r=RT)
                    cos = trig[:, 6, :].rearrange("p (r d) -> p r d", r=RT)
                    for n, table in enumerate((ropeq, ropek)):
                        g = [headg[:, n, 32 * a:32 * a + 32].unsqueeze(1).to_broadcast([P, RT, 32]) for a in range(2)]
                        for a in range(2):
                            dve.tensor_tensor(table[:, 0, :, 32 * a:32 * a + 32], cos, g[a], ALU.mult)
                            ins = dve.scalar_tensor_tensor(out=table[:, 1, :, 32 * a:32 * a + 32], in0=sin,
                                                           scalar=1.0 if a else -1.0, in1=g[1 - a],
                                                           op0=ALU.mult, op1=ALU.mult)
                    link(ins)
                if u >= 7:
                    k = u - 7
                    if k < 12:
                        scores(k)
                    if 2 <= k < 6:
                        dve.wait_ge(stream_evac, 6 + k - 1)
                        conv(2 * (k - 2))
                        conv(2 * (k - 2) + 1)
                    if k in (5, 9):
                        r = (k - 5) // 4
                        i = 4 * r
                        link(dve.reciprocal(rec[:, 0:8], sums[:, 2 * i:2 * i + 8]))
                        dve.wait_ge(pv_ready, i + 4)
                        dve.tensor_tensor(xn[:, r, 0:512].rearrange("p (h d) -> p h d", d=AD),
                                          ps[:, 7, :].rearrange("p (h d) -> p h d", d=AD),
                                          rec[:, 0:8].unsqueeze(2).to_broadcast([P, AH, AD]), ALU.mult)\
                            .then_inc(o_evac, 1)
                    if k in (11, 13):
                        r = (k - 11) // 2
                        den = small[:, 64 + 4 * r:68 + 4 * r]
                        link(dve.scalar_tensor_tensor(out=rec[:, 8:12], in0=den, scalar=-1.0, in1=den,
                                                      op0=ALU.mult, op1=ALU.max))
                        link(dve.tensor_tensor(rec[:, 8:12], rec[:, 8:12], small[:, 56 + 4 * r:60 + 4 * r], ALU.max))
                        link(dve.reciprocal(rec[:, 12:16], rec[:, 8:12]))
                        y = xn[:, r, 512:1024]
                        y3 = y.rearrange("p (h d) -> p h d", d=BD)
                        dve.wait_ge(pv_ready, 10 + 2 * r)
                        dve.tensor_tensor(y3, ps[:, 7, :].rearrange("p (h d) -> p h d", d=BD),
                                          rec[:, 12:16].unsqueeze(2).to_broadcast([P, BH, BD]), ALU.mult)\
                            .then_inc(mh_ready, 1)
                        dve.wait_ge(mh_ready, r + 1)
                        head_sum(r, BH, BD)
                        dve.wait_ge(ob_ready, 1)
                        link(dve.tensor_tensor(y3, y3, head_rstd(r, BH, BD), ALU.mult))
                        link(dve.tensor_tensor(y, y, gml[:, :], ALU.mult))
                        dve.tensor_tensor(y, y, z1[:, r, 4, :], ALU.mult).then_inc(y_ready, 1)
            turned(T_Y0)

            def merge(b):
                v = slice(2 * b, 2 * b + 2)
                flat = lambda s: s[:, v, :].rearrange("p a b -> p (a b)")
                if b >= 2:
                    dve.wait_ge(merged_lo, b - 1)
                dve.tensor_tensor(sc[:, b % 2, :], ps[:, 4 + b, :], flat(sga), ALU.mult)
                link(dve.tensor_tensor(pr[:, b % 2, :], ps[:, b, :], flat(sgb), ALU.mult))
                dve.tensor_tensor(sc[:, b % 2, :], sc[:, b % 2, :], pr[:, b % 2, :], ALU.add)\
                    .then_inc(merged_sum, 1)

            def merged_rest(b):
                v = slice(2 * b, 2 * b + 2)
                flat = lambda s: s[:, v, :].rearrange("p a b -> p (a b)")
                dve.wait_ge(merged_hi, b + 1)
                h, l = (hhi[:, b, :], hlo[:, b, :]) if b < 2 else (flat(xhi), flat(xlo))
                dve.tensor_tensor(l, sc[:, b % 2, :], h, ALU.subtract).then_inc(merged_lo, 1)

            for m in range(2):
                lo(PROJ + 3 + 2 * m)
                lo(PROJ + 4 + 2 * m)
                dve.wait_ge(unit_used, PROJ + 2 * m + 2)
                merge(2 * m)
                merge(2 * m + 1)
                merged_rest(2 * m)
                merged_rest(2 * m + 1)

            def two(u):
                lo(u)
                lo(u + 1)

            two(WO[0] + 3)
            for r in range(RT):
                residual(R_WO0, WO[0] + 3, 1.0, r, (4, 0))
                scaled(N_FFN, res, xn, r)
            turned(T_FFN)
            two(FFU[0] + 1)

            ffn(0, FFU[0], 2)
            for r in range(RT):
                residual(R_FF0, FFU[0] + 32, 1.0, r)
                scaled(N_FIN, res, res, r)
                scaled(N_F1, res, xn, r)

            for L in range(2):
                turned(T_F1 + 5 * L)
                two(FFU[1 + 2 * L] + 1)
                ffn(1 + 2 * L, FFU[1 + 2 * L], 2)
                u = MIXU[L]
                for r in range(RT):
                    residual(R_F1 + 3 * L, FFU[1 + 2 * L] + 32, 0.5, r)
                    scaled(N_M0 + 4 * L, res, xn, r)
                turned(T_M0 + 5 * L)
                two(u + 1)
                eb, tb, i0 = 2 + 10 * L, 8 * L, IT0[L]

                def heads_rest(tt, bank, dst, src, g):
                    dve.wait_ge(heads_hi, tb + tt + 1)
                    dve.scalar_tensor_tensor(out=dst, in0=ps[:, bank, :].rearrange("p (a b) -> p a b", b=SEQ),
                                             scalar=1.0 if g is None else colg[:, g:g + 1], in1=src,
                                             op0=ALU.mult, op1=ALU.subtract).then_inc(heads_lo, 1)

                def head_scale(e, v, n, copied):
                    dve.wait_ge(stream_evac, STREAM0[f"mix{L}"] + copied)
                    v3 = v.rearrange("p (h d) -> p h d", d=HD)
                    return dve.tensor_tensor(v3, v3, head_rstd(e, n, HD), ALU.mult)

                def differential_norm(r):
                    dve.wait_ge(o_copied, 4 + r)
                    y3 = xn[:, r, 0:SW].rearrange("p (h d) -> p h d", d=2 * HD)
                    link(dve.tensor_tensor(y3, y3, head_rstd(22 + r, DH, 2 * HD), ALU.mult))
                    dve.tensor_tensor(y3, y3, gsub[:, :].unsqueeze(1).to_broadcast([P, DH, 2 * HD]), ALU.mult)\
                        .then_inc(y_ready, 1)

                for m in range(8):
                    if m < 7:
                        lo(u + m + 3)
                    s = m // 2
                    if m == 3:
                        for r in range(RT):
                            scaled(N_MEM0 + 4 * L, xn, xn, r)
                    if m in (4, 6):
                        for tt in (m - 4, m - 3):
                            heads_rest(tt, 4 + tt % 4,
                                       qk_lo[tt // 2][:, tt % 2, :].rearrange("p (a b) -> p a b", b=SEQ),
                                       qkT[:, 2 * tt:2 * tt + 2, :], (0 if tt < 3 else 1) if L == 0 else None)
                    if m % 2 and s < 3:
                        for r in range(RT):
                            head_sum(eb + 2 * s + r, 8, HD)
                        for r in range(RT):
                            v = z2[:, r, 512 * s:512 * s + 512]
                            ins = head_scale(eb + 2 * s + r, v, 8, 2 * s + r + 1)
                            if L == 1:
                                link(ins)
                                parts = [[(0, 512, ropeq)], [(0, 256, ropeq), (256, 512, ropek)],
                                         [(0, 512, ropek)]][s]
                                for a, b, table in parts:
                                    ins = rotate(v[:, a:b], (b - a) // HD, table[:, 0, r, :], table[:, 1, r, :],
                                                 rt1[:, a:b], rt2[:, a:b])
                            ins.then_inc(zn_ready, 1)
                for tt in (4, 5):
                    heads_rest(tt, tt, qk_lo[2][:, tt % 2, :].rearrange("p (a b) -> p a b", b=SEQ),
                               qkT[:, 2 * tt:2 * tt + 2, :], 1 if L == 0 else None)
                lo(u + 10)
                if L == 0:
                    dve.wait_ge(toep_ready, 1)
                for k in range(N_IT + 3):
                    if k < N_IT:
                        scores(i0 + k)
                    if 1 <= k <= N_IT:
                        combine(i0 + k - 1)
                    if k in (8, 14):
                        r = (k - 8) // 6
                        i = i0 + 6 * r
                        o = ps[:, 6:8, :].rearrange("p a b -> p (a b)")[:, 0:SW]
                        if L == 0:
                            dve.wait_ge(p_ready, SOFT[i + 5])
                            link(dve.reciprocal(rec[:, 16:28], sums[:, 2 * i:2 * i + 12]))
                            dve.wait_ge(pv_ready, i + 6)
                            dve.tensor_tensor(xn[:, r, 0:SW].rearrange("p (h d) -> p h d", d=HD),
                                              o.rearrange("p (h d) -> p h d", d=HD),
                                              rec[:, 16:28].unsqueeze(2).to_broadcast([P, SH, HD]), ALU.mult)\
                                .then_inc(o_copied, 1)
                        else:
                            dve.wait_ge(pv_ready, i + 6)
                            dve.tensor_copy(xn[:, r, 0:SW], o).then_inc(o_copied, 1)
                    if k in (3, 4):
                        turned(T_MEM0 + 5 * L, range(2 * (k - 3), 2 * (k - 3) + 2))
                    if k in (3, 9):
                        for r in range(RT):
                            head_sum(eb + (6 if k == 3 else 8) + r, MH, HD)
                    if k == 5:
                        for r in range(RT):
                            head_scale(eb + 6 + r, z2[:, r, 3 * SW:ZW], MH, 9 + r).then_inc(zn_ready, 1)
                    if k == 10:
                        for r in range(RT):
                            head_scale(eb + 8 + r, kv[:, r, 0:MW], MH, 11 + r).then_inc(zn_ready, 1)
                    if k == 11:
                        heads_rest(6, 3, qm_lo, qmT, 2 + 2 * L)
                        heads_rest(7, 2, km_lo, kmT, 3 + 2 * L)
                    for k0, c in AHEAD:
                        if k - 1 in (k0, k0 + 1):
                            lo(u + c, k - 1 - k0)
                    if L == 1 and k in (12, 15):
                        head_sum(22 + (k - 12) // 3, DH, 2 * HD, SW)
                    if L == 1 and k in (13, 16):
                        differential_norm((k - 13) // 3)
                i = i0 + 12
                dve.wait_ge(p_ready, SOFT[i + 3])
                link(dve.reciprocal(rec[:, 28:36], sums[:, 2 * i:2 * i + 8]))
                dve.wait_ge(pv_ready, i + 4)
                dve.tensor_tensor(xn[:, :, SW:DM].rearrange("p r (h d) -> p r h d", d=HD),
                                  ps[:, 6, :].rearrange("p (r h d) -> p r h d", r=RT, d=HD),
                                  rec[:, 28:36].rearrange("p (r h) -> p r h", r=RT).unsqueeze(3)
                                  .to_broadcast([P, RT, MH, HD]), ALU.mult).then_inc(o_copied, 1)
                turned(T_Y1 + 5 * L)
                two(WO[1 + L] + 3)
                for r in range(RT):
                    residual(R_WO1 + 3 * L, WO[1 + L] + 3, 1.0, r)
                    scaled(N_F2 + 4 * L, res, xn, r)
                turned(T_F2 + 5 * L)
                two(FFU[2 + 2 * L] + 1)
                if L == 0:
                    ffn(2, FFU[2], 2)
                    for r in range(RT):
                        residual(R_F2, FFU[2] + 32, 0.5, r)
                        scaled(N_F3, res, xn, r)
                else:
                    ffn(4, FFU[4], 1)
                    for r in range(RT):
                        residual(R_F4, FFU[4] + 32, 0.5, r)

        @block.tensor
        def _(pe):
            def three(o, stat, mov, start, stop):
                pe.matmul(o, stat[0], mov[0], start=start, stop=False)
                pe.matmul(o, stat[0], mov[1], start=False, stop=False)
                return pe.matmul(o, stat[1], mov[0], start=False, stop=stop)

            def w(slot, a, n):
                return whi[:, slot, a:a + n], wlo[:, slot, a:a + n]

            def x(k, a=0, n=SEQ):
                return xhi[:, k, a:a + n], xlo[:, k, a:a + n]

            def turn(T, src, n=None, y=None):
                for r in range(RT):
                    if n is None:
                        pe.wait_ge(y[0], y[1] + r + 1)
                    for b in range(4):
                        if n is not None and b % 2 == 0:
                            pe.wait_ge(xn_ready, 2 * place(n, r) + b // 2 + 1)
                        bank = TURN_BANKS.get(T, range(4))[b]
                        for c in (2 * b, 2 * b + 1):
                            a = 256 * (c % 2) + P * r
                            ins = pe.transpose(ps[:, bank, a:a + P], src[:, r, P * c:P * c + P], ident)
                        if r == RT - 1:
                            ins.then_inc(tr_ps, 1)

            def narrow(u, slot, bank, T=None):
                pe.wait_ge(lo_done, u + 1)
                for n in range(2):
                    for k in range(KC):
                        if T is not None and n == 0 and k % 2 == 0:
                            pe.wait_ge(xlo_done, 4 * T + k // 2 + 1)
                        ins = three(ps[:, bank, 256 * n:256 * n + 256], w(slot, 256 * k + P * n, P), x(k),
                                    k == 0, k == KC - 1)
                ins.then_inc(unit_used, 1)

            def wide(u, half, banks, T=None, free=None):
                if u == 0:
                    pe.wait_ge(half_lo, 1)
                else:
                    pe.wait_ge(lo_done, u + 1)
                for r in range(RT):
                    if free and half == 0 and free[r]:
                        pe.wait_ge(*free[r])
                    for k in range(4):
                        if u == 0 and r == 0 and k == 2:
                            pe.wait_ge(lo_done, 1)
                        if T is not None and r == 0 and k % 2 == 0:
                            pe.wait_ge(xlo_done, 4 * T + (4 * half + k) // 2 + 1)
                        ins = three(ps[:, banks[r], :], x(4 * half + k, P * r, P), w(u % 3, 512 * k, 512),
                                    half == 0 and k == 0, half == 1 and k == 3)
                ins.then_inc(unit_used, 1)

            def wide_part(u, half, r, bank, free):
                if r == 0:
                    pe.wait_ge(lo_done, u + 1)
                if free:
                    pe.wait_ge(*free)
                for k in range(4):
                    ins = three(ps[:, bank, :], x(4 * half + k, P * r, P), w(u % 3, 512 * k, 512),
                                half == 0 and k == 0, half == 1 and k == 3)
                if r == RT - 1:
                    ins.then_inc(unit_used, 1)

            def down(u, slot, banks, first, left):
                pe.wait_ge(lo_done, u + 1)
                for r in range(RT):
                    for c in range(2):
                        for n in range(2):
                            ins = three(ps[:, banks[r] + n, :], left(c, r), w(slot, 1024 * c + 512 * n, 512),
                                        first and c == 0, False)
                ins.then_inc(unit_used, 1)

            def last_two(u, banks, lefts, ready):
                for r in range(RT):
                    for k in range(2):
                        if r == 0:
                            pe.wait_ge(*ready[k])
                            pe.wait_ge(lo_done, u + k + 1)
                        for n in range(2):
                            for c in range(2):
                                ins = three(ps[:, banks[r] + n, :], lefts[k](c, r),
                                            w((u + k) % 3, 1024 * c + 512 * n, 512), False, k == 1 and c == 1)
                            if k == 1 and (r, n) < (1, 1):
                                ins.then_inc(acc_ready, 1)
                        if r == 1:
                            ins.then_inc(unit_used, 1)

            def hidden(par):
                return lambda c, r: (hhi[:, par, 256 * c + P * r:256 * c + P * r + P],
                                     hlo[:, par, 256 * c + P * r:256 * c + P * r + P])

            def ffn(f, u0, T):
                j0 = STEPS * f

                def gate_up(J, u, slot, par, T=None, wait=True):
                    if wait:
                        pe.wait_ge(silu_done, J - 1)
                    narrow(u, slot, 2 * par, T)
                    if wait:
                        pe.wait_ge(h_mul, J - 1)
                    narrow(u + 1, (slot + 1) % 3, 2 * par + 1)

                def down_step(J, u, slot, par, first=False):
                    pe.wait_ge(h_ready, J + 1)
                    down(u, slot, (4, 6), first, hidden(par))

                gate_up(j0, u0, u0 % 3, 0, T, False)
                gate_up(j0 + 1, u0 + 2, (u0 + 2) % 3, 1, None, False)
                down_step(j0, u0 + 4, (u0 + 4) % 3, 0, first=True)
                with pe.Fori(0, (STEPS - 3) // 2) as i:
                    for k in range(2):
                        u = u0 + 5 + 3 * k
                        gate_up(i * 2 + (j0 + 2 + k), i * 6 + u, u % 3, k)
                        down_step(i * 2 + (j0 + 1 + k), i * 6 + (u + 2), (u + 2) % 3, 1 - k)
                gate_up(j0 + 10, u0 + 29, (u0 + 29) % 3, 0)
                last_two(u0 + 31, (4, 6), (hidden(1), hidden(0)), [(h_ready, j0 + 10), (h_ready, j0 + 11)])

            def item_scores(i):
                kind, r, a, L = ITEMS[i]
                nk = SEQ if kind == "X" else P * (r + 1)
                j = i - IT0[L] if L >= 0 else i
                if 0 < j < 13:
                    pe.wait_ge(sc_read, i)
                if L >= 0 and j > 13:
                    pe.wait_ge(p_ready, SOFT[i - 2])
                if i == 8:
                    pe.wait_ge(qkb_ready, 1)
                for e in range(2):
                    o = ps[:, s_bank(i) + e, 0:nk]
                    if kind == "M":
                        lhs, rhs = qkb[:, 2 * a + e, P * r:P * r + P], qkb[:, BH + 2 * a + e, 0:nk]
                        ins = pe.matmul(o, lhs, rhs, start=True, stop=True)
                        continue
                    v = slice(HD * e, HD * e + HD)
                    q, k, ql, kl, ka = {"A": (qT, kT, a_lo[0], a_lo[1], a), "X": (qmT, kmT, qm_lo, km_lo, a)}.get(
                        kind, (qkT, qkT, qk_lo[a // 4], qk_lo[(6 + a) // 4], 6 + a))
                    if kind == "X":
                        ql, kl = ql[v, a, P * r:P * r + P], kl[v, a, 0:nk]
                    else:
                        ql = ql[v, a % 4 // 2, 256 * (a % 2) + P * r:256 * (a % 2) + P * r + P]
                        kl = kl[v, ka % 4 // 2, 256 * (ka % 2):256 * (ka % 2) + nk]
                    ins = three(o, (q[v, a, P * r:P * r + P], ql), (k[v, ka, 0:nk], kl), True, True)
                ins.then_inc(sc_ready, 1)

            def item_turn(i):
                kind, r, a, L = ITEMS[i]
                nb = 2 if kind == "X" else r + 1
                if kind == "M":
                    pe.wait_ge(sc_read, i + 1)
                elif kind == "D":
                    pe.wait_ge(comb_ready, DIFF[i])
                else:
                    pe.wait_ge(p_ready, SOFT[i])
                if L < 0:
                    bank = 6
                    if i > 0:
                        pe.wait_ge(pT_evac, i)
                else:
                    bank = 4 + i % 2
                    if i - IT0[L] >= 2:
                        pe.wait_ge(pT_evac, i - 1)
                for e in range(1 if kind == "D" else 2):
                    for b in range(nb):
                        if kind == "M":
                            src = lw[:, 2 * a + e, P * (r + b):P * (r + b) + P]
                        elif kind == "D":
                            src = comb[:, i % 2, P * b:P * b + P]
                        else:
                            src = pr[:, i % 2, 256 * e + P * b:256 * e + P * b + P]
                        c = P * (e * nb + b)
                        ins = pe.transpose(ps[:, bank, c:c + P], src, ident)
                ins.then_inc(pT_ready, 1)

            def item_pv(i):
                kind, r, a, L = ITEMS[i]
                nb = 2 if kind == "X" else r + 1
                pe.wait_ge(pT_evac, i + 1)
                if i in (4, 8):
                    pe.wait_ge(o_evac, i // 4)
                if i == 10:
                    pe.wait_ge(mh_ready, 1)
                if L >= 0 and i - IT0[L] in (6, 12):
                    pe.wait_ge(o_copied, 3 * L + (i - IT0[L]) // 6)
                for e in range(1 if kind == "D" else 2):
                    h = a if kind == "D" else 2 * a + e
                    size = P if kind in "MD" else HD
                    o0 = size * h + (MW * r if kind == "X" else 0)
                    bank, col = (7, o0) if L < 0 else (6 + o0 // 512, o0 % 512)
                    for b in range(nb):
                        v = {"A": z1[:, b, 2, :], "M": z1[:, b, 3, :], "X": kv[:, b, MW:2 * MW],
                             "R": z2[:, b, 2 * SW:3 * SW], "D": z2[:, b, 2 * SW:3 * SW]}[kind]
                        c = P * (e * nb + b)
                        ins = pe.matmul(ps[:, bank, col:col + size], pT[:, i % 2, c:c + P],
                                        v[:, size * h:size * h + size], start=(b == 0), stop=(b == nb - 1))
                ins.then_inc(pv_ready, 1)

            pe.wait_ge(ident_full, 16)
            turn(T_MIX, xn, N_MIX)
            pe.wait_ge(xlo_done, 4 * T_MIX + 4)
            tiles = 0
            for u in range(PROJ):
                free = lambda n: (stream_evac, n - 3) if n >= 4 else None
                if QKB <= u < VB or GA <= u:
                    if free(tiles):
                        pe.wait_ge(*free(tiles))
                    narrow(u, u % 3, tiles % 4)
                    tiles += 1
                else:
                    wide(u, u % 2, (tiles % 4, (tiles + 1) % 4), None, (free(tiles), free(tiles + 1)))
                    tiles += 2 * (u % 2)
                if u == 0:
                    pe.wait_ge(wif_lo, 1)
                    for r in range(RT):
                        for k in range(KC):
                            for part in range(2):
                                ins = pe.matmul(ps[:, 4, 16 * r:16 * r + 16], x(k, P * r, P)[part], wifs[:, k, :],
                                                start=k == 0 and part == 0, stop=k == KC - 1 and part == 1)
                    ins.then_inc(gate_ps, 1)
                    pe.wait_ge(bias_full, 48)
                    pe.transpose(ps[:, 5, 0:32], cwr[:, :], ident[0:32, 0:32]).then_inc(gate_ps, 1)
                if u == 2:
                    pe.wait_ge(cst_full, 16)
                    pe.wait_ge(gate_dve, 3)
                    tri, ones = cst[:, C_TRI:C_TRI + P], cst[:, C_ONE:C_ONE + P]
                    pe.matmul(ps[:, 4, 64:68], tri, small[:, 80:84], start=True, stop=True)
                    pe.matmul(ps[:, 4, 68:72], ones, small[:, 80:84], start=True, stop=False)
                    pe.matmul(ps[:, 4, 68:72], tri, small[:, 84:88], start=False, stop=True).then_inc(gate_ps, 1)
                if u == 3:
                    pe.wait_ge(gate_dve, 5)
                    for h in range(BH):
                        for r in range(RT):
                            c = 256 * (h % 2) + P * r
                            ins = pe.matmul(ps[:, 6 + h // 2, c:c + P], ones, diag[:, r, h, :], start=True, stop=True)
                    ins.then_inc(gate_ps, 1)
                if u in (5, 6):
                    s = u - 5
                    pe.wait_ge(rope_ready, 2 * s + 2)
                    pe.wait_ge(gate_dve, 7)
                    for b in range(2):
                        for c in (2 * b, 2 * b + 1):
                            for r in range(RT):
                                a = 256 * (c % 2) + P * r
                                ins = pe.transpose(ps[:, 4 + 2 * s + b, a:a + P], z1[:, r, s, P * c:P * c + P], ident)
                        ins.then_inc(qk_ps, 1)
                if u == 7:
                    pe.wait_ge(qk_sb, 4)
                    pe.wait_ge(qk_lo_done, 4)
                if u >= 7:
                    k = u - 7
                    if k < 12:
                        item_scores(k)
                    if 1 <= k <= 12:
                        item_turn(k - 1)
                    if 2 <= k <= 13:
                        item_pv(k - 2)
            pe.wait_ge(stream_evac, 22)
            turn(T_Y0, xn, y=(y_ready, 0))
            for m in range(4):
                u = PROJ + m
                pe.wait_ge(lo_done, u + 1)
                for n in range(4):
                    bank = 4 - 4 * (m % 2) + 2 * (m // 2) + n // 2
                    for k in range(4):
                        kk = k + 4 * (m % 2)
                        if n == 0 and k % 2 == 0:
                            pe.wait_ge(xlo_done, 4 * T_Y0 + kk // 2 + 1)
                        ins = three(ps[:, bank, 256 * (n % 2):256 * (n % 2) + 256], w(u % 3, 512 * k + P * n, P), x(kk),
                                    k == 0, k == 3)
                ins.then_inc(unit_used, 1)

            def merged(m):
                def left(c, r):
                    k = 2 * m + c
                    if m < 2:
                        a = 256 * c + P * r
                        return hhi[:, m, a:a + P], hlo[:, m, a:a + P]
                    return x(k, P * r, P)
                return left

            for m in range(2):
                pe.wait_ge(merged_lo, 2)
                down(WO[0] + m, (WO[0] + m) % 3, (4, 0), m == 0, merged(m))
            last_two(WO[0] + 2, (4, 0), (merged(2), merged(3)), [(merged_lo, 3), (merged_lo, 4)])
            turn(T_FFN, xn, N_FFN)

            def out_product(L):
                def left(m):
                    return lambda c, r: x(2 * m + c, P * r, P)

                ready = [(xlo_done, 4 * (T_Y1 + 5 * L) + m + 1) for m in range(4)]
                for m in range(2):
                    pe.wait_ge(*ready[m])
                    down(WO[1 + L] + m, (WO[1 + L] + m) % 3, (4, 6), m == 0, left(m))
                last_two(WO[1 + L] + 2, (4, 6), (left(2), left(3)), ready[2:])

            ffn(0, FFU[0], T_FFN)
            for L in range(2):
                T = T_F1 + 5 * L
                turn(T, xn, N_F1 if L == 0 else N_F3)
                ffn(1 + 2 * L, FFU[1 + 2 * L], T)
                T = T_M0 + 5 * L
                turn(T, xn, N_M0 if L == 0 else N_M1)
                u, base, tb, zb, i0 = MIXU[L], STREAM0[f"mix{L}"], 8 * L, 10 * L, IT0[L]

                def turn_heads(tt, bank, src, c0, ready):
                    pe.wait_ge(zn_ready, ready)
                    if 4 <= tt < 6:
                        pe.wait_ge(heads_lo, tb + tt - 3)
                    for c in range(2):
                        for r in range(RT):
                            a = 256 * c + P * r
                            ins = pe.transpose(ps[:, bank, a:a + P], src[:, r, c0 + P * c:c0 + P * c + P], ident)
                    ins.then_inc(tr_heads, 1)

                def turn_part(T, b, src):
                    for c in (2 * b, 2 * b + 1):
                        for r in range(RT):
                            a = 256 * (c % 2) + P * r
                            ins = pe.transpose(ps[:, TURN_BANKS[T][b], a:a + P], src[:, r, P * c:P * c + P], ident)
                    ins.then_inc(tr_ps, 1)

                for s in range(4):
                    free = [(stream_evac, base + 2 * s + r - 3) if 2 * s + r >= 4 else None for r in range(RT)]
                    for half in range(2):
                        wide(u + 2 * s + half, half, ((2 * s + 2) % 4, (2 * s + 3) % 4), T if s == 0 else None, free)
                    if s == 3:
                        wide_part(u + 8, 0, 0, 2, (stream_evac, base + 5))
                    if s >= 1:
                        for b in range(2):
                            tt = 2 * (s - 1) + b
                            turn_heads(tt, 4 + tt % 4, z2, 256 * tt, zb + 2 * s)
                wide_part(u + 8, 0, 1, 3, (stream_evac, base + 6))
                T = T_MEM0 + 5 * L
                for k in range(N_IT + 3):
                    if k == 0:
                        pe.wait_ge(heads_lo, tb + 6)
                    if k < 2:
                        pe.wait_ge(stream_evac, base + 7 + k)
                    if k == 12:
                        pe.wait_ge(heads_lo, tb + 8)
                    if k < N_IT:
                        item_scores(i0 + k)
                    if 2 <= k < N_IT + 2:
                        item_turn(i0 + k - 2)
                    if k >= 3:
                        item_pv(i0 + k - 3)
                    if k < 2:
                        wide_part(u + 9, 1, k, 2 + k, None)
                    if k == 2:
                        for b in range(2):
                            pe.wait_ge(xn_ready, 2 * place(N_MEM0 + 4 * L, 1) + 2)
                            pe.wait_ge(stream_evac, base + 9 + b)
                            turn_part(T, b, xn)
                    if k == 3:
                        for b in (2, 3):
                            pe.wait_ge(xlo_done, 4 * T + b - 1)
                            turn_part(T, b, xn)
                    if k in MEM_AT:
                        n = MEM_AT.index(k)
                        wide_part(MEMU[L] + n // 2, n // 2, n % 2, 2 + n % 2, (xlo_done, 4 * T + min(n + 3, 4)))
                    if k == 10:
                        pe.wait_ge(stream_evac, base + 12)
                        turn_heads(6, 3, z2, 3 * SW, zb + 8)
                        turn_heads(7, 2, kv, 0, zb + 10)
                    if k >= 17:
                        pe.wait_ge(*((y_ready, 4) if L else (o_copied, 3 * L + 2)))
                        pe.wait_ge(stream_evac, base + 12)
                        turn_part(T + 1, k - 17, xn)
                turn_part(T + 1, 2, xn)
                pe.wait_ge(o_copied, 3 * L + 3)
                turn_part(T + 1, 3, xn)
                out_product(L)
                T = T_F2 + 5 * L
                turn(T, xn, N_F2 if L == 0 else N_F4)
                ffn(2 + 2 * L, FFU[2 + 2 * L], T)


_INS = ["x", "norm_mix_g", "w_in", "conv_w", "b_igate", "b_fgate", "mlstm_norm_g", "w_proj_a", "w_proj_b", "w_out",
        "norm_ffn_g", "w_gate_up", "w_down", "norm_final_g", "mem_2", "positions_2", "ffn1_norm_2", "ffn1_w_gate_2",
        "ffn1_w_up_2", "ffn1_w_down_2", "mix_norm_2", "mem_norm_2", "w_in_2", "w_mem_kv_2", "mem_q_norm_2",
        "mem_k_norm_2", "w_out_2", "a_q_norm_2", "a_k_norm_2", "a_rel_bias_2", "b_q_norm_2", "b_k_norm_2",
        "b_lambda_q1_2", "b_lambda_k1_2", "b_lambda_q2_2", "b_lambda_k2_2", "b_subln_2", "ffn2_norm_2",
        "ffn2_w_gate_2", "ffn2_w_up_2", "ffn2_w_down_2"]


def kernel(**inputs):
    import concourse.bacc as bacc
    from concourse.bass_utils import run_bass_kernel_spmd

    nc = bacc.Bacc("TRN2", target_bir_lowering=False, num_devices=1)
    arrays, aps = {}, {}
    given = {name: inputs[name] for name in _INS}
    given["consts"] = shape_constants()
    for name, a in given.items():
        a = np.ascontiguousarray(a)
        arrays[f"in_{name}"] = a
        aps[name] = nc.dram_tensor(f"in_{name}", a.shape, mybir.dt.from_np(a.dtype), kind="ExternalInput").ap()
    out = nc.dram_tensor("out", (1, SEQ, DM), F32, kind="ExternalOutput").ap()
    build(nc, aps, out)
    r = run_bass_kernel_spmd(nc, [arrays], core_ids=[0])
    return r.results[0]["out"]
```
